# Optimizing a Trainium2 kernel written in Bass

```python
import math
import jax, jax.numpy as jnp
from jax import lax
import numpy as np

D_MODEL = 1024
BATCH = 1
SEQ = 256
DEPTH = 1

POOL_WIDTH = D_MODEL // 2
POOL_WINDOWS = (2, 4, 8, 16)
POOL_GROUPS = len(POOL_WINDOWS)
POOL_GC = POOL_WIDTH // POOL_GROUPS
HEAD_DIM = 64
ATTN_HEADS = (D_MODEL // 2) // HEAD_DIM
ATTN_WIDTH = ATTN_HEADS * HEAD_DIM
MOBA_BLOCK = 256
MOBA_TOPK = 3
QUERY_CHUNK = 64
ROPE_THETA = 500000.0
ROT_DIM = HEAD_DIM // 4
N_BRANCH = 2
IN_WIDTH = 2 * POOL_WIDTH + 4 * ATTN_WIDTH + N_BRANCH * D_MODEL
EPS = 1e-6


def rms_norm(x, g):
    xf = x.astype(jnp.float32)
    y = xf * lax.rsqrt(jnp.mean(xf * xf, axis=-1, keepdims=True) + EPS)
    return (y * g.astype(jnp.float32)).astype(x.dtype)

def partial_rope(x):
    S_ = x.shape[1]
    half = ROT_DIM // 2
    pos = jnp.arange(S_, dtype=jnp.float32)
    inv_freq = ROPE_THETA ** (-jnp.arange(0, ROT_DIM, 2, dtype=jnp.float32) / ROT_DIM)
    ang = pos[:, None] * inv_freq[None, :]
    cos = jnp.cos(ang)[None, :, None, :].astype(x.dtype)
    sin = jnp.sin(ang)[None, :, None, :].astype(x.dtype)
    x1 = x[..., :half]
    x2 = x[..., half:ROT_DIM]
    return jnp.concatenate([x1 * cos - x2 * sin, x2 * cos + x1 * sin, x[..., ROT_DIM:]], axis=-1)

def multiscale_pool(u, w_grp, scale):
    B_, S_, _ = u.shape
    ug = u.reshape(B_, S_, POOL_GROUPS, POOL_GC)
    uf = ug.astype(jnp.float32)
    cs = lax.cumsum(uf, axis=1)
    cs = jnp.concatenate([jnp.zeros_like(cs[:, :1]), cs], axis=1)
    t = jnp.arange(S_)
    means = []
    for g, w in enumerate(POOL_WINDOWS):
        hi = t + 1
        lo = jnp.maximum(t + 1 - w, 0)
        cnt = (hi - lo).astype(jnp.float32)[None, :, None]
        means.append((cs[:, hi, g] - cs[:, lo, g]) / cnt)
    d = (jnp.stack(means, axis=2) - uf).astype(u.dtype)
    y = jnp.einsum('bsgc,gcd->bsgd', d, w_grp).reshape(B_, S_, POOL_WIDTH)
    return y * scale

def moba_attention(q, k, v):
    B_, S_, H, Dh = q.shape
    q = q.transpose(0, 2, 1, 3)
    k = k.transpose(0, 2, 1, 3)
    v = v.transpose(0, 2, 1, 3)
    nb = -(-S_ // MOBA_BLOCK)
    s_pad = nb * MOBA_BLOCK
    pad = ((0, 0), (0, 0), (0, s_pad - S_), (0, 0))
    kb = jnp.pad(k, pad).reshape(B_, H, nb, MOBA_BLOCK, Dh)
    vb = jnp.pad(v, pad).reshape(B_, H, nb, MOBA_BLOCK, Dh)
    kmean = jnp.mean(kb.astype(jnp.float32), axis=3)
    n_sel = min(MOBA_TOPK, nb)
    nq = S_ // QUERY_CHUNK
    q_chunks = q.reshape(B_, H, nq, QUERY_CHUNK, Dh).transpose(2, 0, 1, 3, 4)
    scale = Dh ** -0.5
    bi = jnp.arange(B_)[:, None, None, None]
    hi = jnp.arange(H)[None, :, None, None]
    blk_ids = jnp.arange(nb)
    kr = jnp.arange(MOBA_BLOCK)

    def one_chunk(args):
        ci, qc = args
        q0 = ci * QUERY_CHUNK
        qblk = q0 // MOBA_BLOCK
        qpos = q0 + jnp.arange(QUERY_CHUNK)
        gate = jnp.einsum('bhqd,bhnd->bhqn', qc.astype(jnp.float32), kmean)
        gate = jnp.where(blk_ids < qblk, gate, -jnp.inf)
        _, sel = lax.top_k(gate, n_sel)
        sel_ok = sel < qblk
        ksel = kb[bi, hi, sel]
        vsel = vb[bi, hi, sel]
        s_sel = jnp.einsum('bhqd,bhqkjd->bhqkj', qc, ksel).astype(jnp.float32) * scale
        s_sel = jnp.where(sel_ok[..., None], s_sel, -jnp.inf)
        s_sel = s_sel.reshape(B_, H, QUERY_CHUNK, n_sel * MOBA_BLOCK)
        kown = lax.dynamic_index_in_dim(kb, qblk, axis=2, keepdims=False)
        vown = lax.dynamic_index_in_dim(vb, qblk, axis=2, keepdims=False)
        kpos = qblk * MOBA_BLOCK + kr
        s_own = jnp.einsum('bhqd,bhjd->bhqj', qc, kown).astype(jnp.float32) * scale
        s_own = jnp.where(kpos[None, :] <= qpos[:, None], s_own, -jnp.inf)
        p = jax.nn.softmax(jnp.concatenate([s_sel, s_own], axis=-1), axis=-1).astype(v.dtype)
        p_sel = p[..., :n_sel * MOBA_BLOCK].reshape(B_, H, QUERY_CHUNK, n_sel, MOBA_BLOCK)
        p_own = p[..., n_sel * MOBA_BLOCK:]
        return (jnp.einsum('bhqkj,bhqkjd->bhqd', p_sel, vsel)
                + jnp.einsum('bhqj,bhjd->bhqd', p_own, vown))

    out = lax.map(one_chunk, (jnp.arange(nq), q_chunks))
    return out.transpose(1, 0, 3, 2, 4).reshape(B_, S_, H * Dh)

def first_inputs(seed: int = 0) -> dict:
    key = jax.random.key(seed)
    ks = jax.random.split(key, 14)
    D = D_MODEL
    nrm = jax.random.normal
    return {
        "x": nrm(ks[0], (BATCH, SEQ, D), jnp.float32),
        "c": nrm(ks[1], (BATCH, D), jnp.float32),
        "w_ada": nrm(ks[2], (DEPTH, D, 3 * D), jnp.float32) * (0.3 * D ** -0.5),
        "b_ada": nrm(ks[3], (DEPTH, 3 * D), jnp.float32) * 0.01,
        "g_norm": 1.0 + 0.05 * nrm(ks[4], (DEPTH, D), jnp.float32),
        "w_in": nrm(ks[5], (DEPTH, D, IN_WIDTH), jnp.float32) * D ** -0.5,
        "w_pool_grp": nrm(ks[6], (DEPTH, POOL_GROUPS, POOL_GC, POOL_GC), jnp.float32) * POOL_GC ** -0.5,
        "pool_scale": 1.0 + 0.1 * nrm(ks[7], (DEPTH, POOL_WIDTH), jnp.float32),
        "w_pool_up": nrm(ks[8], (DEPTH, POOL_WIDTH, D), jnp.float32) * POOL_WIDTH ** -0.5,
        "w_attn_up": nrm(ks[9], (DEPTH, ATTN_WIDTH, D), jnp.float32) * ATTN_WIDTH ** -0.5,
        "w_out": nrm(ks[10], (DEPTH, D, D), jnp.float32) * D ** -0.5,
        "g_final": 1.0 + 0.05 * nrm(ks[11], (D,), jnp.float32),
    }

def first_block(x, c, w_ada, b_ada, g_norm, w_in, w_pool_grp, pool_scale, w_pool_up, w_attn_up, w_out, g_final):
    B_, S_, D = x.shape
    splits = np.cumsum([POOL_WIDTH, POOL_WIDTH, ATTN_WIDTH, ATTN_WIDTH, ATTN_WIDTH, ATTN_WIDTH, D_MODEL]).tolist()
    for l in range(DEPTH):
        mod = c @ w_ada[l] + b_ada[l]
        shift, scl, gate = jnp.split(mod, 3, axis=-1)
        h = rms_norm(x, g_norm[l]) * (1.0 + scl[:, None, :]) + shift[:, None, :]
        proj = h @ w_in[l]
        u_pool, z_pool, q, k, v, z_attn, m_pool, m_attn = jnp.split(proj, splits, axis=-1)
        y_pool = multiscale_pool(u_pool, w_pool_grp[l], pool_scale[l]) * jax.nn.silu(z_pool)
        y_pool = y_pool @ w_pool_up[l]
        q = partial_rope(q.reshape(B_, S_, ATTN_HEADS, HEAD_DIM))
        k = partial_rope(k.reshape(B_, S_, ATTN_HEADS, HEAD_DIM))
        v = v.reshape(B_, S_, ATTN_HEADS, HEAD_DIM)
        y_attn = moba_attention(q, k, v) * jax.nn.silu(z_attn)
        y_attn = y_attn @ w_attn_up[l]
        merged = jax.nn.sigmoid(m_pool) * y_pool + jax.nn.sigmoid(m_attn) * y_attn
        x = x + gate[:, None, :] * (merged @ w_out[l])
    return rms_norm(x, g_final)


D_MIX = D_MODEL
RET_HEADS = 4
RET_DK = 128
RET_DV = 128
RET_CHUNK = 128
NSA_HEADS = 8
NSA_KV_GROUPS = 2
NSA_HPG = NSA_HEADS // NSA_KV_GROUPS
NSA_DH = 64
CMP_LEN = 32
CMP_STRIDE = 16
CMP_HID = 256
SEL_BLOCK = 64
SEL_TOPN = 16
WINDOW = 512
Q_BLOCK = 128
FORCED_SCORE = 1e9
ROPE_THETA_2 = 10000.0
PEER_HEADS = 8
PEER_NKEYS = 128
PEER_EXPERTS = PEER_NKEYS * PEER_NKEYS
PEER_TOPK = 16
PEER_DQ = 256
PEER_DHALF = PEER_DQ // 2
PEER_TOK_BLOCK = 128
NORM_EPS = 1e-6
KV_COLS = NSA_KV_GROUPS * NSA_DH
IN_SPLITS = (RET_HEADS * RET_DK, RET_HEADS * RET_DK, RET_HEADS * RET_DV, RET_HEADS * RET_DV,
             NSA_HEADS * NSA_DH, KV_COLS, KV_COLS, KV_COLS, KV_COLS, KV_COLS, KV_COLS,
             NSA_HEADS * 3)
IN_COLS = sum(IN_SPLITS)


def _rms_norm(x, g):
    xf = x.astype(jnp.float32)
    y = xf * lax.rsqrt(jnp.mean(xf * xf, axis=-1, keepdims=True) + NORM_EPS)
    return (y * g.astype(jnp.float32)).astype(x.dtype)

def _modulate(h, shift, scale):
    return h * (1.0 + scale[:, None, :]) + shift[:, None, :]

def _rope(x, pos):
    d = x.shape[-1]
    inv = ROPE_THETA_2 ** (-jnp.arange(0, d, 2, dtype=jnp.float32) / d)
    ang = pos.astype(jnp.float32)[:, None] * inv[None, :]
    cos = jnp.cos(ang)[None, :, None, :].astype(x.dtype)
    sin = jnp.sin(ang)[None, :, None, :].astype(x.dtype)
    x1, x2 = jnp.split(x, 2, axis=-1)
    return jnp.concatenate([x1 * cos - x2 * sin, x2 * cos + x1 * sin], axis=-1)

def _masked_softmax(s, mask):
    s = jnp.where(mask, s, -jnp.inf)
    m = jnp.max(s, axis=-1, keepdims=True)
    m = jnp.where(jnp.isfinite(m), m, 0.0)
    e = jnp.where(mask, jnp.exp(s - m), 0.0)
    return e / jnp.maximum(jnp.sum(e, axis=-1, keepdims=True), jnp.finfo(jnp.float32).tiny)

def _retention(q, k, v, g):
    B, S, H, DK = q.shape
    DV = v.shape[-1]
    C = RET_CHUNK
    nc = S // C
    f32 = jnp.float32
    log_g = jnp.log1p(-jnp.exp2(-5.0 - jnp.arange(H, dtype=f32)))
    n = jnp.arange(C, dtype=f32)
    diff = n[:, None] - n[None, :]
    causal = diff >= 0
    dmat = jnp.where(causal[None], jnp.exp(jnp.where(causal, diff, 0.0)[None] * log_g[:, None, None]), 0.0)
    qc = q.astype(f32).reshape(B, nc, C, H, DK)
    kc = (k.astype(f32) * DK ** -0.5).reshape(B, nc, C, H, DK)
    vc = v.astype(f32).reshape(B, nc, C, H, DV)
    scores = jnp.einsum('bcnhk,bcmhk->bchnm', qc, kc) * dmat[None, None]
    inner = jnp.einsum('bchnm,bcmhv->bcnhv', scores, vc)
    zeta = jnp.exp((C - 1 - n)[None, :] * log_g[:, None])
    kv = jnp.einsum('bcmhk,bcmhv,hm->cbhkv', kc, vc, zeta)
    cdecay = jnp.exp(C * log_g)[None, :, None, None]

    def step(state, kv_c):
        return cdecay * state + kv_c, state

    _, s_prev = lax.scan(step, jnp.zeros((B, H, DK, DV), f32), kv)
    xi = jnp.exp((n + 1.0)[None, :] * log_g[:, None])
    cross = jnp.einsum('bcnhk,cbhkv,hn->bcnhv', qc, s_prev, xi)
    y = (inner + cross).reshape(B, S, H, DV)
    mu = jnp.mean(y, axis=-1, keepdims=True)
    var = jnp.mean((y - mu) ** 2, axis=-1, keepdims=True)
    y = (y - mu) * lax.rsqrt(var + NORM_EPS)
    y = jax.nn.silu(g.astype(f32)) * y
    return y.reshape(B, S, H * DV).astype(q.dtype)

def _compress(kraw, pe, w1, b1, w2):
    B, S, G, DH = kraw.shape
    ncb = (S - CMP_LEN) // CMP_STRIDE + 1
    idx = jnp.arange(ncb)[:, None] * CMP_STRIDE + jnp.arange(CMP_LEN)[None, :]
    blk = kraw[:, idx] + pe[None, None, :, None, :]
    blk = blk.transpose(0, 1, 3, 2, 4).reshape(B, ncb, G, CMP_LEN * DH)
    return jax.nn.gelu(blk @ w1 + b1) @ w2

def _nsa(q, k_c, v_c, k_s, v_s, k_w, v_w, gate_logits, pe_k, pe_v, wk1, bk1, wk2, wv1, bv1, wv2):
    B, S = q.shape[:2]
    G, HPG, DH = NSA_KV_GROUPS, NSA_HPG, NSA_DH
    f32 = jnp.float32
    kc = _compress(k_c, pe_k, wk1, bk1, wk2)
    vc = _compress(v_c, pe_v, wv1, bv1, wv2)
    ncb = kc.shape[1]
    nsel = S // SEL_BLOCK
    n_top = min(SEL_TOPN, nsel)
    nqb = S // Q_BLOCK
    cmp_start = jnp.arange(ncb) * CMP_STRIDE
    cmp_end = cmp_start + CMP_LEN - 1
    sel_start = jnp.arange(nsel) * SEL_BLOCK
    overlap = jnp.clip(jnp.minimum(cmp_start[:, None] + CMP_LEN, sel_start[None, :] + SEL_BLOCK)
                       - jnp.maximum(cmp_start[:, None], sel_start[None, :]), 0).astype(f32) / CMP_STRIDE
    ks_g = k_s.reshape(B, nsel, SEL_BLOCK, G, DH).transpose(0, 3, 1, 2, 4)
    vs_g = v_s.reshape(B, nsel, SEL_BLOCK, G, DH).transpose(0, 3, 1, 2, 4)
    kw_pad = jnp.pad(k_w, ((0, 0), (WINDOW, 0), (0, 0), (0, 0)))
    vw_pad = jnp.pad(v_w, ((0, 0), (WINDOW, 0), (0, 0), (0, 0)))
    qg = q.reshape(B, nqb, Q_BLOCK, G, HPG, DH).swapaxes(0, 1)
    gg = gate_logits.reshape(B, nqb, Q_BLOCK, G, HPG, 3).swapaxes(0, 1)
    scale = DH ** -0.5
    gather = jax.vmap(jax.vmap(lambda tbl, ix: tbl[ix]))
    blk_ids = jnp.arange(nsel)

    def body(args):
        qb, qblk, gblk = args
        t = qb * Q_BLOCK + jnp.arange(Q_BLOCK)
        s_c = jnp.einsum('bqghd,bngd->bghqn', qblk, kc).astype(f32) * scale
        p_c = _masked_softmax(s_c, cmp_end[None, :] <= t[:, None])
        o_c = jnp.einsum('bghqn,bngd->bqghd', p_c.astype(vc.dtype), vc)
        imp = jnp.einsum('bghqn,nj->bgqj', p_c, overlap)
        cur = t // SEL_BLOCK
        forced = (blk_ids[None, :] == 0) | (blk_ids[None, :] == cur[:, None]) | (blk_ids[None, :] == cur[:, None] - 1)
        imp = jnp.where(forced, FORCED_SCORE, imp)
        imp = jnp.where(blk_ids[None, :] <= cur[:, None], imp, -jnp.inf)
        top_v, top_i = lax.top_k(imp, n_top)
        ksel = gather(ks_g, top_i)
        vsel = gather(vs_g, top_i)
        pos = top_i[..., None] * SEL_BLOCK + jnp.arange(SEL_BLOCK)
        m_s = jnp.isfinite(top_v)[..., None] & (pos <= t[None, None, :, None, None])
        s_s = jnp.einsum('bqghd,bgqnkd->bghqnk', qblk, ksel).astype(f32) * scale
        p_s = _masked_softmax(s_s.reshape(B, G, HPG, Q_BLOCK, n_top * SEL_BLOCK),
                              m_s.reshape(B, G, 1, Q_BLOCK, n_top * SEL_BLOCK))
        o_s = jnp.einsum('bghqm,bgqmd->bqghd', p_s.astype(vsel.dtype),
                         vsel.reshape(B, G, Q_BLOCK, n_top * SEL_BLOCK, DH))
        kwb = lax.dynamic_slice_in_dim(kw_pad, qb * Q_BLOCK, Q_BLOCK + WINDOW, axis=1)
        vwb = lax.dynamic_slice_in_dim(vw_pad, qb * Q_BLOCK, Q_BLOCK + WINDOW, axis=1)
        sp = qb * Q_BLOCK - WINDOW + jnp.arange(Q_BLOCK + WINDOW)
        m_w = (sp[None, :] >= 0) & (sp[None, :] <= t[:, None]) & (sp[None, :] > t[:, None] - WINDOW)
        s_w = jnp.einsum('bqghd,bkgd->bghqk', qblk, kwb).astype(f32) * scale
        p_w = _masked_softmax(s_w, m_w)
        o_w = jnp.einsum('bghqk,bkgd->bqghd', p_w.astype(vwb.dtype), vwb)
        gate = jax.nn.sigmoid(gblk.astype(f32))
        out = gate[..., 0:1] * o_c + gate[..., 1:2] * o_s + gate[..., 2:3] * o_w
        return out.astype(qblk.dtype)

    out = lax.map(body, (jnp.arange(nqb), qg, gg))
    return out.swapaxes(0, 1).reshape(B, S, NSA_HEADS * DH)

def _peer(h, w_q, subkeys, w_down, w_up):
    B, S, D = h.shape
    TB = PEER_TOK_BLOCK
    nb = S // TB
    hb = h.reshape(B, nb, TB, D).swapaxes(0, 1)

    def body(hblk):
        q = (hblk @ w_q).reshape(B, TB, PEER_HEADS, 2, PEER_DHALF)
        s = jnp.einsum('btphd,phnd->btphn', q, subkeys).astype(jnp.float32)
        v, i = lax.top_k(s, PEER_TOPK)
        cand = (v[..., 0, :, None] + v[..., 1, None, :]).reshape(B, TB, PEER_HEADS, PEER_TOPK * PEER_TOPK)
        cidx = (i[..., 0, :, None] * PEER_NKEYS + i[..., 1, None, :]).reshape(B, TB, PEER_HEADS, PEER_TOPK * PEER_TOPK)
        tv, tj = lax.top_k(cand, PEER_TOPK)
        eidx = jnp.take_along_axis(cidx, tj, axis=-1)
        w = jax.nn.softmax(tv, axis=-1)
        u = w_down[eidx]
        a = jax.nn.gelu(jnp.einsum('btd,btpkd->btpk', hblk, u).astype(jnp.float32))
        vv = w_up[eidx]
        return jnp.einsum('btpk,btpkd->btd', (w * a).astype(hblk.dtype), vv)

    out = lax.map(body, hb)
    return out.swapaxes(0, 1).reshape(B, S, D)

def second_inputs(seed: int = 0) -> dict:
    key = jax.random.key(seed)
    ks = jax.random.split(key, 24)
    L = DEPTH

    def nrm(k, shape, s):
        return jax.random.normal(k, shape, jnp.float32) * s

    return {
        "x": nrm(ks[0], (BATCH, SEQ, D_MODEL), 1.0),
        "c": nrm(ks[1], (BATCH, D_MODEL), 1.0),
        "w_ada": nrm(ks[2], (L, D_MODEL, 6 * D_MODEL), 0.5 * D_MODEL ** -0.5),
        "b_ada": nrm(ks[3], (L, 6 * D_MODEL), 0.02),
        "g_norm_mix": 1.0 + nrm(ks[4], (L, D_MODEL), 0.02),
        "w_in": nrm(ks[5], (L, D_MODEL, IN_COLS), D_MODEL ** -0.5),
        "pe_cmp_k": nrm(ks[6], (L, CMP_LEN, NSA_DH), 0.1),
        "pe_cmp_v": nrm(ks[7], (L, CMP_LEN, NSA_DH), 0.1),
        "w_cmp_k1": nrm(ks[8], (L, CMP_LEN * NSA_DH, CMP_HID), (CMP_LEN * NSA_DH) ** -0.5),
        "b_cmp_k1": nrm(ks[9], (L, CMP_HID), 0.02),
        "w_cmp_k2": nrm(ks[10], (L, CMP_HID, NSA_DH), CMP_HID ** -0.5),
        "w_cmp_v1": nrm(ks[11], (L, CMP_LEN * NSA_DH, CMP_HID), (CMP_LEN * NSA_DH) ** -0.5),
        "b_cmp_v1": nrm(ks[12], (L, CMP_HID), 0.02),
        "w_cmp_v2": nrm(ks[13], (L, CMP_HID, NSA_DH), CMP_HID ** -0.5),
        "w_out": nrm(ks[14], (L, D_MIX, D_MODEL), D_MIX ** -0.5),
        "g_norm_ffn": 1.0 + nrm(ks[15], (L, D_MODEL), 0.02),
        "w_peer_q": nrm(ks[16], (L, D_MODEL, PEER_HEADS * PEER_DQ), D_MODEL ** -0.5),
        "peer_subkeys": nrm(ks[17], (L, PEER_HEADS, 2, PEER_NKEYS, PEER_DHALF), PEER_DHALF ** -0.5),
        "peer_down": nrm(ks[18], (L, PEER_EXPERTS, D_MODEL), D_MODEL ** -0.5),
        "peer_up": nrm(ks[19], (L, PEER_EXPERTS, D_MODEL), PEER_HEADS ** -0.5),
        "g_norm_final": 1.0 + nrm(ks[20], (D_MODEL,), 0.02),
    }

def second_block(x, c, w_ada, b_ada, g_norm_mix, w_in, pe_cmp_k, pe_cmp_v, w_cmp_k1, b_cmp_k1, w_cmp_k2,
              w_cmp_v1, b_cmp_v1, w_cmp_v2, w_out, g_norm_ffn, w_peer_q, peer_subkeys, peer_down, peer_up,
              g_norm_final):
    B, S, D = x.shape
    pos = jnp.arange(S)
    split_points = [int(v) for v in np.cumsum(IN_SPLITS)[:-1]]
    for l in range(DEPTH):
        mod = jax.nn.silu(c) @ w_ada[l] + b_ada[l]
        sh1, sc1, ga1, sh2, sc2, ga2 = jnp.split(mod, 6, axis=-1)
        h = _modulate(_rms_norm(x, g_norm_mix[l]), sh1, sc1)
        proj = h @ w_in[l]
        (r_q, r_k, r_v, r_g, n_q, n_kc, n_vc, n_ks, n_vs, n_kw, n_vw, n_gate) = jnp.split(proj, split_points, axis=-1)
        r_q = _rope(r_q.reshape(B, S, RET_HEADS, RET_DK), pos)
        r_k = _rope(r_k.reshape(B, S, RET_HEADS, RET_DK), pos)
        ret_out = _retention(r_q, r_k, r_v.reshape(B, S, RET_HEADS, RET_DV), r_g.reshape(B, S, RET_HEADS, RET_DV))
        kvshape = (B, S, NSA_KV_GROUPS, NSA_DH)
        nsa_out = _nsa(_rope(n_q.reshape(B, S, NSA_HEADS, NSA_DH), pos),
                       _rope(n_kc.reshape(kvshape), pos), n_vc.reshape(kvshape),
                       _rope(n_ks.reshape(kvshape), pos), n_vs.reshape(kvshape),
                       _rope(n_kw.reshape(kvshape), pos), n_vw.reshape(kvshape),
                       n_gate, pe_cmp_k[l], pe_cmp_v[l], w_cmp_k1[l], b_cmp_k1[l], w_cmp_k2[l],
                       w_cmp_v1[l], b_cmp_v1[l], w_cmp_v2[l])
        mix = jnp.concatenate([ret_out, nsa_out], axis=-1) @ w_out[l]
        x = x + ga1[:, None, :] * mix
        h = _modulate(_rms_norm(x, g_norm_ffn[l]), sh2, sc2)
        x = x + ga2[:, None, :] * _peer(h, w_peer_q[l], peer_subkeys[l], peer_down[l], peer_up[l])
    return _rms_norm(x, g_norm_final)


def setup_inputs(seed=0):
    out = dict(first_inputs(seed))
    for name, value in second_inputs(seed + 1).items():
        if name != "x":
            out[name + "_2"] = value
    return out


def reference(
    x, c, w_ada, b_ada, g_norm, w_in, w_pool_grp, pool_scale, w_pool_up, w_attn_up, w_out,
    g_final, c_2, w_ada_2, b_ada_2, g_norm_mix_2, w_in_2, pe_cmp_k_2, pe_cmp_v_2, w_cmp_k1_2,
    b_cmp_k1_2, w_cmp_k2_2, w_cmp_v1_2, b_cmp_v1_2, w_cmp_v2_2, w_out_2, g_norm_ffn_2,
    w_peer_q_2, peer_subkeys_2, peer_down_2, peer_up_2, g_norm_final_2,
):
    x = first_block(
        x, c, w_ada, b_ada, g_norm, w_in, w_pool_grp, pool_scale, w_pool_up, w_attn_up, w_out,
        g_final,
    )
    return second_block(
        x, c_2, w_ada_2, b_ada_2, g_norm_mix_2, w_in_2, pe_cmp_k_2, pe_cmp_v_2, w_cmp_k1_2,
        b_cmp_k1_2, w_cmp_k2_2, w_cmp_v1_2, b_cmp_v1_2, w_cmp_v2_2, w_out_2, g_norm_ffn_2,
        w_peer_q_2, peer_subkeys_2, peer_down_2, peer_up_2, g_norm_final_2,
    )


_drawn_inputs = setup_inputs


def setup_inputs(seed=0):
    import zlib

    import numpy as np

    out = dict(_drawn_inputs(seed))
    spreads = {}
    factors = {'b_ada': 8.0,
     'g_norm': 5.375,
     'pool_scale': 4.367,
     'b_ada_2': 3.038,
     'g_norm_mix_2': 7.641,
     'pe_cmp_k_2': 8.0,
     'pe_cmp_v_2': 7.079,
     'w_cmp_k1_2': 3.254,
     'b_cmp_k1_2': 8.0,
     'w_cmp_k2_2': 3.15,
     'b_cmp_v1_2': 40.959,
     'g_norm_ffn_2': 6.717,
     'g_norm_final_2': 7.839}
    for name, (base, spread) in spreads.items():
        noise = np.random.default_rng([zlib.crc32(name.encode()), seed]).standard_normal(out[name].shape)
        drawn = base * np.exp(spread * noise) if base else spread * noise
        out[name] = __import__('jax').numpy.asarray(drawn.astype(out[name].dtype))
    for name, factor in factors.items():
        out[name] = (out[name] * factor).astype(out[name].dtype)
    return out
```

```python
from contextlib import ExitStack

import numpy as np

import concourse.bass as bass
from concourse import mybir

F32 = mybir.dt.float32
F32R = mybir.dt.float32r
U32 = mybir.dt.uint32
ALU = mybir.AluOpType
ACT = mybir.ActivationFunctionType
AX = mybir.AxisListType.X

P = 128
T = 256
NT = T // P
D = 1024
C = D // P
EPS = 1e-6
PANEL = C * 512
SLOTS = 4
H = 8
NEG = -1e30
LOWEST = -3e38
NCMP = 15
K16 = 16
RAW = 4
SPLIT = 2

STREAM = []
STREAM += [("ada1", p, PANEL, "dve") for p in (2, 3, 0, 1)]
for a, b in ((("in1", 2), ("ada1", 4)), (("in1", 3), ("ada1", 5)), (("in1", 4), ("ada2", 2)), (("in1", 5), ("ada2", 3)),
             (("in1", 0), ("ada2", 0)), (("in1", 1), ("ada2", 1)), (("in1", 6), ("ada2", 8)), (("in1", 7), ("ada2", 9)),
             (("in1", 8), ("ada2", 6)), (("in1", 9), ("ada2", 7))):
    STREAM += [(*a, PANEL, "pe"), (*b, PANEL, "dve")]
STREAM += [("poolup", None, PANEL, "pe"), ("attnup", None, PANEL, "pe"), ("out1", 0, PANEL, "pe"), ("out1", 1, PANEL, "pe")]
STREAM += [("in2", 5, PANEL, "pe"), ("in2b", None, C * 280, "pe"), ("in2", 4, PANEL, "pe"), ("ada2", 4, PANEL, "dve"),
           ("cmpk", None, PANEL, "pe"), ("cmpv", None, PANEL, "pe"), ("in2", 0, PANEL, "pe"), ("ada2", 5, PANEL, "dve"),
           ("in2", 1, PANEL, "pe"), ("ada2", 10, PANEL, "dve"), ("in2", 2, PANEL, "pe"), ("ada2", 11, PANEL, "dve"),
           ("in2", 3, PANEL, "pe")]
STREAM += [("out2", 0, PANEL, "pe"), ("out2", 1, PANEL, "pe")]
STREAM += [("wq", p, PANEL, "pe") for p in range(4)]
STREAM += [("subkeys", None, 2048, "pe")]
AT = {(name, i): n for n, (name, i, _, _) in enumerate(STREAM)}
ADA = [n for n, s in enumerate(STREAM) if s[3] == "dve"]

IN1_LATER = [("in1", 5), ("in1", 0), ("in1", 1), ("in1", 6), ("in1", 7), ("in1", 8), ("in1", 9)]


def ada_after(order, done):
    out = []
    while done[0] < len(ADA) and ADA[done[0]] < order:
        out.append(ADA[done[0]])
        done[0] += 1
    return out


def steps():
    out, ada = [], [0]

    def panel(name, i):
        sums = ada_after(AT[(name, i)], ada)
        for t in range(NT):
            out.append(("proj", name, i, t))
        out.extend(("ada", n) for n in sums)

    def half(name, i, t):
        sums = ada_after(AT[(name, i)], ada)
        out.append(("proj", name, i, t))
        out.extend(("ada", n) for n in sums)

    def heads(first, later):
        for i in range(H + 2):
            if i < H:
                out.append(("score", first + i))
            if i < len(later):
                for item in later[i]:
                    if item[0] == "panel":
                        panel(*item[1:])
                    elif item[0] == "half":
                        half(*item[1:])
                    else:
                        out.append(item)
            if 1 <= i <= H:
                out.append(("pT", first + i - 1))
            if i >= 2:
                out.append(("pv", first + i - 2))

    for n in ada_after(AT[("in1", 2)], ada):
        out.append(("ada", n))
    out.extend(("xT", 0, t, half) for t in range(NT) for half in range(2))
    panel("in1", 2)
    panel("in1", 3)
    out.extend(("qkT", qk, t) for qk in range(2) for t in range(NT))
    panel("in1", 4)
    heads(0, [[("panel", *p)] for p in IN1_LATER])
    for n in ada_after(AT[("poolup", None)], ada):
        out.append(("ada", n))
    out.extend(("poolT", half) for half in range(2))
    out.extend(("pool", t) for t in range(NT))
    out.extend(("oT", t) for t in range(NT))
    out.extend(("upT", t) for t in range(NT))
    out.extend(("up", "poolup", t, half) for t in range(NT) for half in range(2))
    out.extend(("up", "attnup", t, half) for t in range(NT) for half in range(2))
    out.extend(("mT", 0, t, half) for t in range(NT) for half in range(2))
    out.extend(("wout", 0, half, t) for half in range(2) for t in range(NT))
    out.extend(("xT", 1, t, half) for t in range(NT) for half in range(2))
    panel("in2", 5)
    panel("in2b", None)
    panel("in2", 4)
    out.extend(("kvT", kind) for kind in range(4))
    out.extend(("nqT", t) for t in range(NT))
    out.extend(("hid", kv) for kv in range(2))
    out.extend([("cmpK",), ("cmpV",), ("cmpVrep",)])
    out.extend(("cmpS", t) for t in range(NT))
    heads(8, [[("half", "in2", 0, 0)], [("half", "in2", 0, 1)], [("half", "in2", 1, 0)], [("half", "in2", 1, 1)],
              [("rT", 0, 0), ("rT", 0, 1)], [("rT", 1, 0), ("rT", 1, 1)], [("half", "in2", 2, 0)], [("half", "in2", 2, 1)]])
    heads(16, [[("half", "in2", 3, 0)], [("ret", 0), ("ret", 1)], [("retO", 0), ("retO", 1)], [("half", "in2", 3, 1)],
               [("ret", 2), ("ret", 3)], [("retO", 2), ("retO", 3)]])
    for n in ada_after(AT[("out2", 0)], ada):
        out.append(("ada", n))
    out.extend(("cmpT", t) for t in range(NT))
    out.extend(("cmpO", t) for t in range(NT))
    out.extend(("mT", 1, t, half) for t in range(NT) for half in range(2))
    out.extend(("wout", 1, half, t) for half in range(2) for t in range(NT))
    out.extend(("xT", 2, t, half) for t in range(NT) for half in range(2))
    out.extend(("peerq", k) for k in range(8))
    out.extend(("peers", k) for k in range(8))
    return out


STEPS = steps()


USE, full_count, freed_count, turn = {}, [0] * 8, [0] * 8, 0
for s in STEPS:
    if s[0] in ("pv", "cmpO", "retO"):
        continue
    bank = turn % 4
    turn += 1
    USE[s] = (bank, full_count[bank] + 1, freed_count[bank], freed_count[bank] + 1)
    full_count[bank] += 1
    freed_count[bank] += 1


LAST_USE = {}
for s in STEPS:
    if s[0] == "proj":
        LAST_USE[AT[s[1], s[2]]] = s
    elif s[0] == "up":
        LAST_USE[AT[s[1], None]] = s
    elif s[0] == "wout":
        LAST_USE[AT[f"out{s[1] + 1}", s[2]]] = s
    elif s[0] == "hid":
        LAST_USE[AT[("cmpk", "cmpv")[s[1]], None]] = s
    elif s[0] == "peerq":
        LAST_USE[AT["wq", s[1] // 2]] = s
    elif s[0] == "peers":
        LAST_USE[AT["subkeys", None]] = s


def tables():
    f = np.float32
    tok = np.arange(T, dtype=f)

    def rope(theta, rot):
        inv = f(theta) ** (-np.arange(0, rot, 2, dtype=f) / f(rot))
        ang = (tok[:, None] * inv[None, :]).astype(f)
        both = np.stack([np.cos(ang), np.sin(ang)], 1).astype(f)
        return both.reshape(NT, P, 2, rot // 2).transpose(1, 2, 0, 3).reshape(P, -1)

    p = np.arange(P)
    decay = np.zeros((P, 4, 3 * P))
    for h in range(4):
        g = 1.0 - 2.0 ** (-5.0 - h)
        diff = np.arange(T)[None, :] - p[:, None]
        full = np.where(diff >= 0, g ** np.maximum(diff, 0), 0.0) * P ** -0.5
        decay[:, h, :T] = full
        decay[:, h, T:] = full[:, :P]
    mask = np.zeros((P, 3 * P))
    mask[:, :P] = np.where(np.arange(P)[None, :] <= p[:, None], 0.0, NEG)
    mask[:, P:] = np.where(np.arange(T)[None, :] <= p[:, None] + P, 0.0, NEG)
    ok = (np.arange(NCMP)[None, None, :] * 16 + 31 <= (np.arange(NT)[None, :, None] * P + p[:, None, None]))
    bmask = (p[:, None] // 16 == np.arange(8)[None, :])
    sel = ((p[:, None] == np.arange(P)[None, :] % 16) & (p[:, None] < NCMP))
    parts = [("rope1", rope(500000.0, 16)), ("ropeR", rope(10000.0, 128)), ("ropeN", rope(10000.0, 64)),
             ("decay", decay.reshape(P, -1)), ("mask", mask), ("cmpadd", np.where(ok, 0.0, NEG).reshape(P, -1)),
             ("cmpok", ok.reshape(P, -1)), ("bmask", bmask), ("sel", sel)]
    keep = [("ident", np.eye(P)), ("iota", np.broadcast_to(np.arange(P), (P, P))), ("ones", np.ones((P, P)))]
    band = np.zeros((P, NT, 4, T))
    for g, w in enumerate((2, 4, 8, 16)):
        full = np.zeros((T, T))
        for t in range(T):
            lo = max(t + 1 - w, 0)
            full[lo:t + 1, t] = 1.0 / (t + 1 - lo)
            full[t, t] -= 1.0
        band[:, :, g, :] = full.reshape(NT, P, T).transpose(1, 0, 2)
    pack = lambda xs: np.ascontiguousarray(np.concatenate([np.asarray(x, f) for _, x in xs], 1))
    offsets = {}
    for xs in (parts, keep):
        at = 0
        for name, x in xs:
            offsets[name] = (at, x.shape[1])
            at += x.shape[1]
    return pack(parts), pack(keep), np.ascontiguousarray(band.reshape(P, -1), dtype=f), offsets


def program(nc, d, out):
    offsets = d["offsets"]
    with ExitStack() as ctx:
        address = {}

        def sb(name, cols):
            address[name] = (nc.sbuf_base + 31) // 32 * 32
            return ctx.enter_context(nc.sbuf_tensor(name, [P, cols], F32))

        sem = lambda name: ctx.enter_context(nc.semaphore(name))

        G = sb("G", P * T)
        ring = sb("ring", (RAW + 2 * SPLIT) * D)
        x = sb("x", NT * D)
        hT3 = sb("hT3", C * T)
        rows = sb("rows", 3 * D)
        gateA, gfin, gateB = (rows[:, k * D:(k + 1) * D] for k in range(3))
        n_tab, n_keep = d["tab"].shape[1], d["keep"].shape[1]
        tab = sb("tab", n_tab + 1024)
        keep = sb("keep", n_keep)
        small = sb("small", 690)

        over = lambda name, first, off, cols: nc.alloc_sbuf_tensor_at(name, [P, cols], F32R, offset=address[first] + 4 * off)
        gs_r = over("gs_r", "x", 0, 4 * T)
        split_r = over("split_r", "ring", RAW * D, 2 * SPLIT * D)
        h_high_r, h_low_r = over("h_high_r", "rows", 0, C * T), over("h_low_r", "hT3", 0, C * T)
        hot_r = over("hot_r", "tab", 1024, 2048)

        def view(tensor, off, *dims):
            n = int(np.prod(dims))
            v = tensor[:, off:off + n]
            if len(dims) == 1:
                return v
            names = "abcd"[:len(dims)]
            sizes = {names[k]: dims[k] for k in range(1, len(dims))}
            return v.rearrange(f"p ({' '.join(names)}) -> p {' '.join(names)}", **sizes)

        def table(name, *dims):
            at, n = offsets[name]
            return view(keep if name in ("ident", "iota", "ones") else tab, at, *(dims or (n,)))

        slot = [view(G, k * PANEL, PANEL) for k in range(SLOTS)]
        TMP = SLOTS * PANEL
        tmp = lambda off, *dims: view(G, TMP + off, *dims)
        rtm = lambda off, *dims: view(ring, off, *dims)
        ident, ones = table("ident"), table("ones")
        rope1 = table("rope1", 2, NT, 8)
        ropeR = table("ropeR", 2, NT, 64)
        ropeN = table("ropeN", 2, NT, 32)
        decay = table("decay", 4, 3 * P)
        mask = table("mask")
        cmpadd, cmpok = table("cmpadd", NT, NCMP), table("cmpok", NT, NCMP)
        acc = [view(tab, n_tab + 512 * k, 512) for k in range(2)]

        xv = view(x, 0, NT, D)
        hT = [tmp(0, C, T), tmp(0, C, T), view(hT3, 0, C, T)]
        xn = [tmp(12288, NT, D), tmp(9216, NT, D), tmp(9216, NT, D)]
        qk_nat = tmp(2048, 2, NT, 512)
        v_nat = tmp(4096, NT, 512)
        qkT = tmp(5120, 2, 4, T)
        za, eza = tmp(7168, NT, 512), tmp(8192, NT, 512)
        u_nat = tmp(9216, NT, 512)
        zp, ezp = tmp(10240, NT, 512), tmp(11264, NT, 512)
        em = tmp(12288, 2, NT, D)
        merged = [tmp(2048, NT, D), rtm(1536, NT, D)]
        mT = [tmp(5120, C, T), rtm(3584, C, T)]
        pbuf = [rtm(384 * k, 384) for k in range(2)]
        ptbuf = [rtm(768 + 384 * k, 384) for k in range(2)]
        band = rtm(1536, NT, 4, T)
        wgrp = rtm(3584, 4, P)
        pscale = rtm(4096, 512)
        dT = rtm(4608, 4, T)
        upT = [rtm(5632, 4, T), rtm(6656, 4, T)]
        ropet = rtm(7680, 512)
        nq_nat, nqT = tmp(9216, NT, 512), tmp(10240, 4, T)
        kv_nat = tmp(11264, NT, 6, P)
        kv_twice = view(hT3, 0, 4, NT, 2 * P)
        kvT = tmp(12800, 4, 2, T)
        egate = tmp(14848, NT, 24)
        blk = tmp(14912, 2, 16, 2 * NCMP)
        hidT = tmp(15872, 2, 2, 2 * NCMP)
        kcT = tmp(15992, 2, 2, NCMP)
        vcomp = tmp(16056, 2, 64)
        vbd = rtm(5632, H, 64)
        cmps = rtm(6144, NT, H, NCMP)
        pc = rtm(6400, NT, H, 16)
        pcT = rtm(6656, NT, P)
        rpt = [rtm(6912 + 384 * k, 384) for k in range(2)]
        s_at = [0]

        def col(*dims):
            n = int(np.prod(dims))
            v = view(small, s_at[0], *dims)
            s_at[0] += n
            return v

        c1, c2, sc2 = col(8), col(8), col(8)
        b1c, b2c = col(24), col(48)
        gcol = col(3, 8)
        modA, modB = col(3, 8), col(3, 8)
        pe, cb1 = col(2, 16), col(2, 2)
        ss, rstd, half_neg = col(2), col(2), col(8)
        mx, nb, sm, rs = col(2, 2), col(2, 2), col(2, 2), col(2, 2)
        bnv, bst, rr = col(NT, 4, 2), col(6), col(8)
        cm, cs = col(8), col(8)
        w2k, w2v = col(2, P), col(2, 64)
        dummy = col(8)
        assert s_at[0] <= 690, s_at[0]

        qpT = tmp(0, 16, T)
        s_all = tmp(4096, NT, 16, P)
        v16, i16u, i16f = tmp(8192, NT, 16, K16), tmp(8704, NT, 16, K16), tmp(9216, NT, 16, K16)
        cand = tmp(9728, H, K16, K16)
        eq = tmp(11776, H, K16, K16)
        tv = tmp(13824, H, K16)
        tju, tju2 = tmp(13952, H, K16), tmp(14080, H, K16)
        taf = tmp(14208, 2, H, K16)
        sel3 = tmp(14464, 3, NT, P)
        sm8 = tmp(15232, H)
        selT = view(tab, 0, 4, T)
        O1 = [view(hot_r, 512 * k, 4, P) for k in range(2)]
        hot2 = view(tab, 3072, 4, 64)
        O2 = [view(hot_r, 1024 + 512 * k, 4, 2, 64) for k in range(2)]
        wsum = [view(x, 1024 + 256 * k, 4, 64) for k in range(2)]
        gs = [[view(gs_r, 512 * k + 256 * part, T) for part in range(2)] for k in range(2)]
        raw = view(ring, 0, RAW, D)
        wsplit = view(split_r, 0, SPLIT, 2, D)
        h_high = view(h_high_r, 0, C, T)
        h_low = view(h_low_r, 0, C, T)
        x_back, gfin2, fin = view(G, 0, NT, D), view(G, 2 * D, D), view(G, 4 * D, NT, D)
        Gv = view(G, 0, P, T)
        iota = table("iota")

        ps = [ctx.enter_context(nc.psum_tensor(f"bank{b}", [P, 512], F32)) for b in range(8)]
        full = [sem(f"bank{b}_full") for b in range(4)]
        freed = [sem(f"bank{b}_freed") for b in range(4)]
        panel_in = [sem(f"panel_in{k}") for k in range(SLOTS)]
        consts_in, tables_in, band_in = sem("consts_in"), sem("tables_in"), sem("band_in")
        gateA_in, w2_in = sem("gateA_in"), sem("w2_in")
        x_in, twice_ready = sem("x_in"), sem("twice_ready")
        acc_ready = sem("acc_ready")
        dve_chain = sem("dve_chain")
        var_ready, rstd_ready, xn_ready = sem("var_ready"), sem("rstd_ready"), sem("xn_ready")
        c2_exp, half_set = sem("c2_exp"), sem("half_set")
        mod_ready = sem("mod_ready")
        smax, sexp, snorm = sem("smax"), sem("sexp"), sem("snorm")
        pv_done = sem("pv_done")
        o_full, o_freed = sem("o_full"), sem("o_freed")
        y_ready = sem("y_ready")
        merged_ready = sem("merged_ready")
        x_ready = sem("x_ready")
        blk_ready, cmp_ready, cmpe, cmpp = sem("blk_ready"), sem("cmp_ready"), sem("cmpe"), sem("cmpp")
        ret_p, ret_done, gn_var, gn_rstd = sem("ret_p"), sem("ret_done"), sem("gn_var"), sem("gn_rstd")
        sel_ready = sem("sel_ready")
        wexp, wexp_in = sem("wexp"), sem("wexp_in")
        selT_full, selT_ready = sem("selT_full"), sem("selT_ready")
        raw_in = [sem(f"raw_in{k}") for k in range(RAW)]
        high_ready, low_ready = sem("high_ready"), sem("low_ready")
        h_high_ready, h_low_ready = sem("h_high_ready"), sem("h_low_ready")
        col_done, act_credit = sem("col_done"), sem("act_credit")
        hot2_ready = sem("hot2_ready")
        x_saved, x_reloaded = sem("x_saved"), sem("x_reloaded")
        hot_ready, w_full, w_credit = sem("hot_ready"), sem("w_full"), sem("w_credit")
        w_done, w_copied = sem("w_done"), sem("w_copied")
        gs_high, gs_low = sem("gs_high"), sem("gs_low")
        out_ready, stored = sem("out_ready"), sem("stored")
        ring_free = sem("ring_free")

        def bank_to_fill(eng, s):
            b, _, before, _ = USE[s]
            if before:
                eng.wait_ge(freed[b], before)
            return ps[b]

        def bank_full(ins, s):
            ins.then_inc(full[USE[s][0]], 1)

        def bank_read(eng, s):
            b, n, _, _ = USE[s]
            eng.wait_ge(full[b], n)
            return ps[b]

        def bank_free(ins, s):
            ins.then_inc(freed[USE[s][0]], 1)

        def evacuated(eng, s):
            eng.wait_ge(freed[USE[s][0]], USE[s][3])

        def wait_panel(eng, n):
            eng.wait_ge(panel_in[n % SLOTS], 16 * (n // SLOTS + 1))
            return slot[n % SLOTS]

        def panel_used(eng, n):
            if STREAM[n][3] == "dve":
                eng.wait_ge(acc_ready, ADA.index(n) + 1)
            else:
                b, count, _, _ = USE[LAST_USE[n]]
                eng.wait_ge(full[b], count)

        def chained(eng, semaphore):
            count = [0]

            def link(ins):
                count[0] += 1
                ins.then_inc(semaphore, 1)
                eng.wait_ge(semaphore, count[0])
            return link

        block = ctx.enter_context(nc.Block())

        @block.sync
        def _(sp):
            loads = [(c1, d["c1"]), (c2, d["c2"]), (keep[:, :], d["keep"]), (b1c, d["b1"]), (b2c, d["b2"]),
                     (gcol, d["g"]), (pe, d["pe"]), (cb1, d["cb1"])]
            for dst, src in loads:
                sp.dma_start(dst, src).then_inc(consts_in, 16)
            sp.dma_start(xv, d["x"]).then_inc(x_in, 16)
            for n, (name, i, cols, user) in enumerate(STREAM):
                if n >= SLOTS:
                    panel_used(sp, n - SLOTS)
                src = d[name] if i is None else d[name][i]
                sp.dma_start(slot[n % SLOTS][:, 0:cols], src).then_inc(panel_in[n % SLOTS], 16)
                if n == SLOTS - 1:
                    sp.dma_start(tab[:, 0:n_tab], d["tab"]).then_inc(tables_in, 16)
                    sp.dma_start(gateA, d["gate1"].partition_broadcast(P)).then_inc(tables_in, 16)
                    sp.dma_start(gateB, d["gate3"].partition_broadcast(P)).then_inc(tables_in, 16)
                    sp.dma_start(gfin, d["gfin1"].partition_broadcast(P)).then_inc(tables_in, 16)
                if n == 2 * SLOTS:
                    sp.dma_start(band, d["band"]).then_inc(band_in, 16)
                    sp.dma_start(wgrp, d["wgrp"]).then_inc(band_in, 16)
                    sp.dma_start(pscale, d["pscale"].partition_broadcast(P)).then_inc(band_in, 16)
            sp.wait_ge(ring_free, 1)
            for s in range(RAW):
                sp.dma_start(raw[:, s, :], d["down"][s]).then_inc(raw_in[s], 16)
            sp.dma_start(out, xv).then_inc(x_saved, 16)

            def loads(array, it, first):
                for s in range(RAW):
                    sp.wait_ge(low_ready, it * RAW + (first + s + 1 - RAW))
                    src = d[array][bass.ds(it * RAW + s, 1), :, :].rearrange("o p n -> (o p) n")
                    sp.dma_start(raw[:, s, :], src).then_inc(raw_in[s], 16)

            with sp.Fori(1, P // RAW) as it:
                loads("down", it, 0)
            with sp.Fori(0, P // RAW) as it:
                loads("up", it, P)
            sp.wait_ge(col_done, P + 64)
            sp.wait_ge(x_saved, 16)
            sp.dma_start(x_back, out).then_inc(x_reloaded, 16)
            sp.dma_start(gfin2, d["gfin2"].partition_broadcast(P)).then_inc(x_reloaded, 16)
            for t in range(NT):
                sp.wait_ge(out_ready, t + 1)
                sp.dma_start(out[:, t, :], fin[:, t, :]).then_inc(stored, 16)
            sp.wait_ge(stored, 16 * NT)

        @block.gpsimd
        def _(pool):
            pool.memset(half_neg, -0.5).then_inc(half_set, 1)
            pool.wait_ge(half_set, 1)
            for k in range(3):
                pool.wait_ge(var_ready, k + 1)
                pool.tensor_tensor(rstd, ss, half_neg[:, 0:2], ALU.pow).then_inc(rstd_ready, 1)
            evacuated(pool, ("proj", "in2", 5, 0))
            pool.memset(kcT, 0.0)
            for kind, which in enumerate((0, 1, 2, 4)):
                for t in range(NT):
                    evacuated(pool, ("proj", "in2" if which < 4 else "in2b", 5 if which < 4 else None, t))
                    src = kv_nat[:, t, which, :].rearrange("p (g e) -> p g e", g=2)
                    pool.tensor_copy(kv_twice[:, kind, t, :].rearrange("p (g r e) -> p g r e", g=2, r=2),
                                     src.unsqueeze(2).to_broadcast([P, 2, 2, 64])).then_inc(twice_ready, 1)
            pool.wait_ge(gn_var, 1)
            pool.tensor_tensor(rr, cs, half_neg, ALU.pow).then_inc(gn_rstd, 1)
            pool.wait_ge(var_ready, 4)
            pool.tensor_tensor(rstd, ss, half_neg[:, 0:2], ALU.pow).then_inc(rstd_ready, 1)
            with pool.Fori(0, 24) as it:
                for k in range(8):
                    pool.wait_ge(high_ready, it * 8 + (k + 1))
                    pool.tensor_tensor(wsplit[:, k % SPLIT, 1, :], raw[:, k % RAW, :], wsplit[:, k % SPLIT, 0, :].bitcast(F32),
                                       ALU.subtract).then_inc(low_ready, 1)
            pool.wait_ge(var_ready, 5)
            pool.tensor_tensor(rstd, ss, half_neg[:, 0:2], ALU.pow).then_inc(rstd_ready, 1)

        @block.scalar
        def _(act):
            act.wait_ge(consts_in, 16 * 8)
            nc.scalar.activation(sc2, c2, ACT.Exp, scale=-1.0).then_inc(c2_exp, 1)

            def score_exp(hh):
                act.wait_ge(smax, hh + 1)
                k = hh % 2
                for lo, hi, part in ((0, P, 0), (P, 3 * P, 1)):
                    ins = nc.scalar.activation(pbuf[k][:, lo:hi], pbuf[k][:, lo:hi], ACT.Exp, scale=0.125,
                                               bias=nb[:, k, part:part + 1], accum_out=sm[:, k, part:part + 1])
                ins.then_inc(sexp, 1)

            for s in STEPS:
                kind = s[0]
                if kind == "xT" and s[2] == 1:
                    src = bank_read(act, s)
                    blk_n, t, half = s[1:]
                    if half == 0:
                        act.wait_ge(mod_ready, blk_n + 1)
                    for c in range(4):
                        cc = 4 * half + c
                        ins = nc.scalar.activation(hT[blk_n][:, cc, t * P:(t + 1) * P], src[:, c * P:(c + 1) * P],
                                                   ACT.Identity, scale=modA[:, blk_n, cc:cc + 1],
                                                   bias=modB[:, blk_n, cc:cc + 1])
                    bank_free(ins, s)
                elif kind == "proj":
                    _, name, i, t = s
                    if name == "in1" and i in (2, 3):
                        pass
                    elif name == "in1" and i in (4, 0):
                        src = bank_read(act, s)
                        dst = v_nat if i == 4 else u_nat
                        bank_free(nc.scalar.activation(dst[:, t, :], src[:, :], ACT.Copy), s)
                    elif name == "in1" and i in (5, 1):
                        src = bank_read(act, s)
                        z, e = (za, eza) if i == 5 else (zp, ezp)
                        nc.scalar.activation(e[:, t, :], src[:, :], ACT.Exp, scale=-1.0)
                        bank_free(nc.scalar.activation(z[:, t, :], src[:, :], ACT.Copy), s)
                    elif name == "in1":
                        src = bank_read(act, s)
                        dst = em[:, (i - 6) // 2, t, (i % 2) * 512:(i % 2) * 512 + 512]
                        bank_free(nc.scalar.activation(dst, src[:, :], ACT.Exp, scale=-1.0), s)
                    elif name == "in2" and i == 2:
                        src = bank_read(act, s)
                        bank_free(nc.scalar.activation(v_nat[:, t, :], src[:, :], ACT.Copy), s)
                    elif name == "in2" and i == 3:
                        src = bank_read(act, s)
                        nc.scalar.activation(eza[:, t, :], src[:, :], ACT.Exp, scale=-1.0)
                        bank_free(nc.scalar.activation(za[:, t, :], src[:, :], ACT.Copy), s)
                elif kind == "qkT" or kind == "rT":
                    src = bank_read(act, s)
                    dst = qkT[:, s[1], :, s[2] * P:(s[2] + 1) * P]
                    bank_free(nc.scalar.activation(dst, src[:, :].rearrange("p (c n) -> p c n", c=4), ACT.Copy), s)
                elif kind == "nqT":
                    src = bank_read(act, s)
                    dst = nqT[:, :, s[1] * P:(s[1] + 1) * P]
                    bank_free(nc.scalar.activation(dst, src[:, :].rearrange("p (c n) -> p c n", c=4), ACT.Copy), s)
                elif kind == "kvT":
                    src = bank_read(act, s)[:, :].rearrange("p (g n) -> p g n", g=2)
                    dst = kvT[:, s[1], :, :]
                    if s[1] < 2:
                        nc.scalar.activation(dst[0:64, :, :], src[0:64, :, :], ACT.Copy)
                        ins = nc.scalar.activation(dst[64:P, :, 0:T - 1], src[64:P, :, 1:T], ACT.Copy)
                    else:
                        ins = nc.scalar.activation(dst, src, ACT.Copy)
                    bank_free(ins, s)
                elif kind == "score":
                    score_exp(s[1])
                elif kind == "pT":
                    hh = s[1]
                    src = bank_read(act, s)
                    if hh >= 2:
                        act.wait_ge(pv_done, hh - 1)
                    bank_free(nc.scalar.activation(ptbuf[hh % 2], src[:, 0:384], ACT.Copy), s)
                elif kind == "poolT":
                    src = bank_read(act, s)
                    bank_free(nc.scalar.activation(dT[:, 2 * s[1]:2 * s[1] + 2, :],
                                                   src[:, :].rearrange("p (g n) -> p g n", g=2), ACT.Copy), s)
                elif kind in ("oT", "upT"):
                    src = bank_read(act, s)
                    dst = upT[1 if kind == "oT" else 0][:, :, s[1] * P:(s[1] + 1) * P]
                    bank_free(nc.scalar.activation(dst, src[:, :].rearrange("p (c n) -> p c n", c=4), ACT.Copy), s)
                elif kind == "mT":
                    src = bank_read(act, s)
                    _, b, t, half = s
                    dst = mT[b][:, 4 * half:4 * half + 4, t * P:(t + 1) * P]
                    bank_free(nc.scalar.activation(dst, src[:, :].rearrange("p (c n) -> p c n", c=4), ACT.Copy), s)
                elif kind == "hid":
                    src = bank_read(act, s)
                    for hc in range(2):
                        ins = nc.scalar.activation(hidT[:, s[1], hc, :], src[:, hc * 30:hc * 30 + 30],
                                                   ACT.Gelu_apprx_tanh, bias=cb1[:, s[1], hc:hc + 1])
                    bank_free(ins, s)
                elif kind == "cmpK":
                    src = bank_read(act, s)
                    for odd in range(2):
                        rows = slice(64 * odd, 64 * odd + 64)
                        ins = nc.scalar.activation(kcT[rows, :, odd, :],
                                                   src[rows, 0:30].rearrange("p (g n) -> p g n", g=2), ACT.Copy)
                    bank_free(ins, s)
                elif kind == "cmpV":
                    src = bank_read(act, s)
                    bank_free(nc.scalar.activation(vcomp[0:NCMP, :, :], src[0:NCMP, 0:128]
                                                   .rearrange("p (g e) -> p g e", g=2), ACT.Copy), s)
                elif kind == "cmpS" and s[1] == 0:
                    evacuated(act, ("proj", "in2b", None, 1))
                    nc.scalar.activation(egate, egate, ACT.Exp, scale=-1.0).then_inc(cmpe, 1)
                elif kind == "cmpS" and s[1] == 1:
                    act.wait_ge(cmp_ready, 1)
                    nc.scalar.activation(cmps, cmps, ACT.Exp, scale=0.125).then_inc(cmpe, 1)
                elif kind == "cmpT":
                    src = bank_read(act, s)
                    bank_free(nc.scalar.activation(pcT[:, s[1], :], src[:, 0:P], ACT.Copy), s)
                elif kind == "peerq":
                    if s[1] == 0:
                        for t in range(NT):
                            for half in range(2):
                                evacuated(act, ("xT", 2, t, half))
                        nc.scalar.activation(h_high, hT[2], ACT.Copy).then_inc(h_high_ready, 1)
                    src = bank_read(act, s)
                    bank_free(nc.scalar.activation(qpT[:, 2 * s[1]:2 * s[1] + 2, :],
                                                   src[:, :].rearrange("p (g n) -> p g n", g=2), ACT.Copy), s)
                elif kind == "peers":
                    src = bank_read(act, s)
                    t, part = divmod(s[1], 4)
                    bank_free(nc.scalar.activation(s_all[:, t, 4 * part:4 * part + 4, :],
                                                   src[:, :].rearrange("p (g n) -> p g n", g=4), ACT.Copy), s)
                if s == ("wout", 0, 1, 1):
                    act.wait_ge(x_ready, 1)
                    act.dma_start(gateA, d["gate2"].partition_broadcast(P)).then_inc(gateA_in, 16)
                    act.dma_start(w2k, d["w2k"]).then_inc(w2_in, 16)
                    act.dma_start(w2v, d["w2v"]).then_inc(w2_in, 16)

            for k in range(2):
                nc.scalar.activation(dummy[:, k:k + 1], ones[:, k:k + 1], ACT.Gelu_apprx_tanh).then_inc(act_credit, 1)

            def high(k):
                nc.scalar.activation(wsplit[:, k % SPLIT, 0, :], raw[:, k % RAW, :], ACT.Copy).then_inc(high_ready, 1)

            def w_copy(m, k):
                act.wait_ge(w_full, m + 1)
                act.wait_ge(w_done, m + 1)
                src = ps[2 + k % 2][:, :].rearrange("p (t b j) -> p t b j", t=4, b=2)[:, :, 0, :]
                nc.scalar.activation(wsum[k % 2], src, ACT.Copy).then_inc(w_copied, 1)

            def gelus(it, with_w):
                for k in range(8):
                    act.wait_ge(col_done, it * 8 + k + 1)
                    act.wait_ge(raw_in[(k + 2) % RAW], it * (16 * 8 // RAW) + 16 * ((k + 2) // RAW + 1))
                    high(k + 2)
                    nc.scalar.activation(Gv[:, bass.ds(it * 8 + k, 1), :], ps[k % 2][:, 0:T].unsqueeze(1),
                                         ACT.Gelu_apprx_tanh).then_inc(act_credit, 1)
                    if with_w:
                        w_copy(it * 8 + (k - 64), k)

            for n in range(SPLIT):
                act.wait_ge(raw_in[n], 16)
                high(n)
            nc.scalar.activation(dummy[:, 3:4], ones[:, 0:1], ACT.Gelu_apprx_tanh)
            with act.Fori(0, 8) as it:
                gelus(it, False)
            act.wait_ge(wexp_in, 1)
            nc.scalar.activation(sel3[:, 2], sel3[:, 2], ACT.Exp).then_inc(wexp, 1)
            act.wait_ge(selT_ready, 3)
            nc.scalar.activation(dummy[:, 2:3], ones[:, 0:1], ACT.Gelu_apprx_tanh)
            act.wait_ge(x_saved, 16)
            with act.Fori(8, 16) as it:
                gelus(it, True)

            act.wait_ge(w_done, 2 + 64)
            for k in range(2):
                nc.scalar.activation(gs[k][0], Gv[:, k, :], ACT.Copy).then_inc(gs_high, 1)

            def stage(it, k):
                act.wait_ge(col_done, it * 8 + (P + k - 1))
                act.wait_ge(raw_in[k % RAW], it * (16 * 8 // RAW) + 16 * (P // RAW + k // RAW + 1))
                high(k)
                nc.scalar.activation(gs[k % 2][0].unsqueeze(1), Gv[:, bass.ds(it * 8 + k, 1), :], ACT.Copy).then_inc(gs_high, 1)

            for k in range(2, 8):
                stage(0, k)
                w_copy(62 + k, k)
            with act.Fori(1, 8) as it:
                for k in range(8):
                    stage(it, k)
                    w_copy(it * 8 + (62 + k), k)
            for k in range(2):
                w_copy(126 + k, k)
            act.wait_ge(w_done, 2 + 128)
            with act.Fori(8, 16) as it:
                for k in range(8):
                    stage(it, k)

        @block.tensor
        def _(pe_):
            mm = nc.tensor.matmul

            def transposes(s, parts):
                bank = bank_to_fill(pe_, s)
                for k, src in enumerate(parts):
                    ins = nc.tensor.transpose(bank[:, k * P:(k + 1) * P], src, ident)
                bank_full(ins, s)

            def project(s, lhs, rhs, cols):
                bank = bank_to_fill(pe_, s)
                n = len(lhs)
                for c in range(n):
                    ins = mm(bank[:, 0:cols], lhs[c], rhs[c], start=(c == 0), stop=(c == n - 1))
                bank_full(ins, s)

            pe_.wait_ge(consts_in, 16 * 8)
            for s in STEPS:
                kind = s[0]
                if kind == "ada":
                    n = s[1]
                    k = ADA.index(n)
                    bank = bank_to_fill(pe_, s)
                    pe_.wait_ge(acc_ready, k + 1)
                    name, i = STREAM[n][0], STREAM[n][1]
                    gate = (name == "ada1" and i >= 4) or (name == "ada2" and i in (4, 5, 10, 11))
                    if gate:
                        ins = mm(bank[:, :], ones, acc[k % 2], start=True, stop=True)
                    else:
                        for c in range(4):
                            ins = mm(bank[:, c:c + 1], acc[k % 2][:, c * P:(c + 1) * P], ones[:, 0:1], start=True, stop=True)
                    bank_full(ins, s)
                elif kind == "xT":
                    b, t, half = s[1:]
                    if half == 0:
                        pe_.wait_ge(xn_ready, 2 * b + t + 1)
                    transposes(s, [xn[b][:, t, (4 * half + c) * P:(4 * half + c + 1) * P] for c in range(4)])
                elif kind == "proj":
                    _, name, i, t = s
                    b = 0 if name == "in1" else 1
                    n = AT[(name, i)]
                    if name in ("in1", "in2") and t == 0 and (name, i) in (("in1", 2), ("in2", 5)):
                        for tt in range(NT):
                            for half in range(2):
                                evacuated(pe_, ("xT", b, tt, half))
                    w = wait_panel(pe_, n)
                    cols = 280 if name == "in2b" else 512
                    wv = w[:, 0:C * cols].rearrange("p (c n) -> p c n", c=C)
                    project(s, [hT[b][:, c, t * P:(t + 1) * P] for c in range(C)], [wv[:, c, :] for c in range(C)], cols)
                elif kind == "qkT":
                    _, qk, t = s
                    evacuated(pe_, ("proj", "in1", 2 + qk, t))
                    transposes(s, [qk_nat[:, qk, t, c * P:(c + 1) * P] for c in range(4)])
                elif kind == "rT":
                    _, qk, t = s
                    evacuated(pe_, ("proj", "in2", qk, t))
                    transposes(s, [qk_nat[:, qk, t, c * P:(c + 1) * P] for c in range(4)])
                elif kind == "nqT":
                    evacuated(pe_, ("proj", "in2", 4, s[1]))
                    transposes(s, [nq_nat[:, s[1], c * P:(c + 1) * P] for c in range(4)])
                elif kind == "kvT":
                    bank = bank_to_fill(pe_, s)
                    pe_.wait_ge(twice_ready, 6 if s[1] < 3 else 8)
                    for g in range(2):
                        for t in range(NT):
                            ins = nc.tensor.transpose(bank[:, (2 * g + t) * P:(2 * g + t + 1) * P],
                                                      kv_twice[:, s[1], t, g * P:(g + 1) * P], ident)
                    bank_full(ins, s)
                elif kind == "score":
                    hh = s[1]
                    bank = bank_to_fill(pe_, s)
                    h = hh % 8
                    lo = 64 * (h % 2)
                    if hh == 0:
                        for qk in range(2):
                            for t in range(NT):
                                evacuated(pe_, ("qkT", qk, t))
                    if hh == 8:
                        for t in range(NT):
                            evacuated(pe_, ("nqT", t))
                        evacuated(pe_, ("kvT", 2))
                        evacuated(pe_, ("kvT", 3))
                    if hh < 8:
                        q, k = qkT[lo:lo + 64, 0, h // 2, :], qkT[lo:lo + 64, 1, h // 2, :]
                    else:
                        q, k = nqT[lo:lo + 64, h // 2, :], kvT[lo:lo + 64, 2 if hh < 16 else 3, h // 4, :]
                    mm(bank[:, 0:P], q[:, 0:P], k[:, 0:P], start=True, stop=True)
                    bank_full(mm(bank[:, P:3 * P], q[:, P:T], k[:, :], start=True, stop=True), s)
                elif kind == "pT":
                    hh = s[1]
                    pe_.wait_ge(snorm, hh + 1)
                    p_ = pbuf[hh % 2]
                    bank = bank_to_fill(pe_, s)
                    for k in range(3):
                        ins = nc.tensor.transpose(bank[:, k * P:(k + 1) * P], p_[:, k * P:(k + 1) * P], ident)
                    bank_full(ins, s)
                elif kind == "pv":
                    hh = s[1]
                    evacuated(pe_, ("pT", hh))
                    h = hh % 8
                    if hh == 0:
                        for t in range(NT):
                            evacuated(pe_, ("proj", "in1", 4, t))
                    if hh == 8:
                        pe_.wait_ge(o_freed, 2)
                    pt = ptbuf[hh % 2]
                    if hh < 8:
                        v = [v_nat[:, t, h * 64:(h + 1) * 64] for t in range(NT)]
                    else:
                        v = [kv_nat[:, t, 3 if hh < 16 else 5, (h // 4) * 64:(h // 4 + 1) * 64] for t in range(NT)]
                    first = hh in (0, 8)
                    last = hh == 7
                    cols = slice(h * 64, (h + 1) * 64)
                    mm(ps[6][:, cols], pt[:, 0:P], v[0], start=first, stop=last, skip_group_check=True)
                    mm(ps[7][:, cols], pt[:, P:2 * P], v[0], start=first, stop=False, skip_group_check=True)
                    mm(ps[7][:, cols], pt[:, 2 * P:3 * P], v[1], start=False, stop=last, skip_group_check=True)\
                        .then_inc(pv_done, 1)
                elif kind == "poolT":
                    half = s[1]
                    if half == 0:
                        for t in range(NT):
                            evacuated(pe_, ("proj", "in1", 0, t))
                        pe_.wait_ge(band_in, 48)
                    bank = bank_to_fill(pe_, s)
                    for k in range(2):
                        g = 2 * half + k
                        mm(bank[:, k * T:(k + 1) * T], u_nat[:, 0, g * P:(g + 1) * P], band[:, 0, g, :],
                           start=True, stop=False, skip_group_check=True)
                        ins = mm(bank[:, k * T + P:(k + 1) * T], u_nat[:, 1, g * P:(g + 1) * P], band[:, 1, g, P:T],
                                 start=False, stop=True, skip_group_check=True)
                    bank_full(ins, s)
                elif kind == "pool":
                    t = s[1]
                    evacuated(pe_, ("poolT", 0))
                    evacuated(pe_, ("poolT", 1))
                    bank = bank_to_fill(pe_, s)
                    for g in range(4):
                        ins = mm(bank[:, g * P:(g + 1) * P], dT[:, g, t * P:(t + 1) * P], wgrp[:, g, :], start=True, stop=True)
                    bank_full(ins, s)
                elif kind == "oT":
                    t = s[1]
                    pe_.wait_ge(y_ready, t + 1)
                    transposes(s, [za[:, t, c * P:(c + 1) * P] for c in range(4)])
                elif kind == "upT":
                    t = s[1]
                    pe_.wait_ge(y_ready, NT + t + 1)
                    transposes(s, [zp[:, t, c * P:(c + 1) * P] for c in range(4)])
                elif kind == "up":
                    _, name, t, half = s
                    src = upT[0 if name == "poolup" else 1]
                    evacuated(pe_, ("upT" if name == "poolup" else "oT", t))
                    w = wait_panel(pe_, AT[(name, None)]).rearrange("p (c n) -> p c n", c=4)
                    project(s, [src[:, c, t * P:(t + 1) * P] for c in range(4)],
                            [w[:, c, half * 512:(half + 1) * 512] for c in range(4)], 512)
                elif kind == "mT":
                    _, b, t, half = s
                    if half == 0:
                        pe_.wait_ge(merged_ready, 2 * b + t + 1)
                    transposes(s, [merged[b][:, t, (4 * half + c) * P:(4 * half + c + 1) * P] for c in range(4)])
                elif kind == "wout":
                    _, b, half, t = s
                    if half == 0:
                        evacuated(pe_, ("mT", b, t, 0))
                        evacuated(pe_, ("mT", b, t, 1))
                    w = wait_panel(pe_, AT[(f"out{b + 1}", half)]).rearrange("p (c n) -> p c n", c=C)
                    project(s, [mT[b][:, c, t * P:(t + 1) * P] for c in range(C)], [w[:, c, :] for c in range(C)], 512)
                elif kind == "hid":
                    kv = s[1]
                    pe_.wait_ge(blk_ready, kv + 1)
                    w = wait_panel(pe_, AT[("cmpk" if kv == 0 else "cmpv", None)]).rearrange("p (c n) -> p c n", c=16)
                    bank = bank_to_fill(pe_, s)
                    for hc in range(2):
                        for i in range(16):
                            ins = mm(bank[:, hc * 30:hc * 30 + 30], w[:, i, hc * P:(hc + 1) * P], blk[:, kv, i, :],
                                     start=(i == 0), stop=(i == 15))
                    bank_full(ins, s)
                elif kind == "cmpK":
                    evacuated(pe_, ("hid", 0))
                    pe_.wait_ge(w2_in, 32)
                    bank = bank_to_fill(pe_, s)
                    for hc in range(2):
                        ins = mm(bank[:, 0:30], w2k[:, hc, :], hidT[:, 0, hc, :],
                                 start=(hc == 0), stop=(hc == 1))
                    bank_full(ins, s)
                elif kind == "cmpV":
                    evacuated(pe_, ("hid", 1))
                    bank = bank_to_fill(pe_, s)
                    for g in range(2):
                        for hc in range(2):
                            ins = mm(bank[0:NCMP, g * 64:(g + 1) * 64], hidT[:, 1, hc, g * NCMP:(g + 1) * NCMP],
                                     w2v[:, hc, :], start=(hc == 0), stop=(hc == 1))
                    bank_full(ins, s)
                elif kind == "cmpVrep":
                    evacuated(pe_, ("cmpV",))
                    pe_.wait_ge(tables_in, 64)
                    bank = bank_to_fill(pe_, s)
                    bank_full(mm(bank[:, 0:P], table("sel")[0:NCMP, :], vcomp[0:NCMP, :, :].rearrange("p g e -> p (g e)"),
                                 start=True, stop=True), s)
                elif kind == "cmpS":
                    t = s[1]
                    evacuated(pe_, ("cmpK",))
                    evacuated(pe_, ("nqT", t))
                    bank = bank_to_fill(pe_, s)
                    for pair in range(H // 2):
                        ins = mm(bank[:, pair * 2 * NCMP:(pair + 1) * 2 * NCMP], nqT[:, pair, t * P:(t + 1) * P],
                                 kcT[:, pair // 2, :, :].rearrange("p o n -> p (o n)"), start=True, stop=True)
                    bank_full(ins, s)
                elif kind == "ret":
                    h = s[1]
                    if h == 0:
                        for qk in range(2):
                            for t in range(NT):
                                evacuated(pe_, ("rT", qk, t))
                    bank = bank_to_fill(pe_, s)
                    q, k = qkT[:, 0, h, :], qkT[:, 1, h, :]
                    mm(bank[:, 0:T], k[:, 0:P], q, start=True, stop=True)
                    bank_full(mm(bank[:, T:3 * P], k[:, P:T], q[:, P:T], start=True, stop=True), s)
                elif kind == "retO":
                    h = s[1]
                    pe_.wait_ge(ret_p, h + 1)
                    if h == 0:
                        for t in range(NT):
                            evacuated(pe_, ("proj", "in2", 2, t))
                    r = rpt[h % 2]
                    c = slice(h * P, (h + 1) * P)
                    mm(ps[4][:, c], r[:, 0:P], v_nat[:, 0, c], start=True, stop=True, skip_group_check=True)
                    mm(ps[5][:, c], r[:, P:T], v_nat[:, 0, c], start=True, stop=False, skip_group_check=True)
                    mm(ps[5][:, c], r[:, T:3 * P], v_nat[:, 1, c], start=False, stop=True, skip_group_check=True)\
                        .then_inc(ret_done, 1)
                elif kind == "cmpT":
                    t = s[1]
                    pe_.wait_ge(cmpp, 1)
                    bank = bank_to_fill(pe_, s)
                    bank_full(nc.tensor.transpose(bank[:, 0:P], pc[:, t, :, :].rearrange("p h n -> p (h n)"), ident), s)
                elif kind == "cmpO":
                    t = s[1]
                    evacuated(pe_, ("cmpT", t))
                    evacuated(pe_, ("cmpVrep",))
                    mm(ps[6 + t][:, :], pcT[:, t, :], vbd.rearrange("p h e -> p (h e)"), start=False, stop=True,
                       skip_group_check=True).then_inc(o_full, 1)
                elif kind == "peerq":
                    k = s[1]
                    if k == 0:
                        for tt in range(NT):
                            for half in range(2):
                                evacuated(pe_, ("xT", 2, tt, half))
                    w = wait_panel(pe_, AT[("wq", k // 2)]).rearrange("p (c n) -> p c n", c=C)
                    bank = bank_to_fill(pe_, s)
                    for g in range(2):
                        lo = (k % 2) * T + g * P
                        for c in range(C):
                            ins = mm(bank[:, g * T:(g + 1) * T], w[:, c, lo:lo + P], hT[2][:, c, :],
                                     start=(c == 0), stop=(c == C - 1))
                    bank_full(ins, s)
                elif kind == "peers":
                    t, part = divmod(s[1], 4)
                    w = wait_panel(pe_, AT[("subkeys", None)])[:, 0:2048].rearrange("p (g n) -> p g n", g=16)
                    bank = bank_to_fill(pe_, s)
                    for g in range(4):
                        if t == 0 and g % 2 == 0:
                            evacuated(pe_, ("peerq", 2 * part + g // 2))
                        ins = mm(bank[:, g * P:(g + 1) * P], qpT[:, 4 * part + g, t * P:(t + 1) * P], w[:, 4 * part + g, :],
                                 start=True, stop=True)
                    bank_full(ins, s)

            for b in range(4):
                pe_.wait_ge(freed[b], freed_count[b])
            pe_.wait_ge(o_freed, 4)

            def down(it, k):
                w = [wsplit[:, k % SPLIT, part, :].rearrange("p (c i) -> p c i", c=C) for part in range(2)]
                pe_.wait_ge(act_credit, it * 8 + (k + 1))
                pe_.wait_ge(high_ready, it * 8 + (k + 1))
                o = ps[k % 2][:, 0:T]
                for c in range(C):
                    mm(o, w[0][:, c, :], h_high[:, c, :], start=(c == 0), stop=False)
                    mm(o, w[0][:, c, :], h_low[:, c, :], start=False, stop=False)
                pe_.wait_ge(low_ready, it * 8 + (k + 1))
                for c in range(C):
                    ins = mm(o, w[1][:, c, :], h_high[:, c, :], start=False, stop=(c == C - 1))
                ins.then_inc(col_done, 1)

            def weights(m, k):
                pe_.wait_ge(hot_ready, m + 1)
                pe_.wait_ge(w_credit, m + 1)
                for t in range(4):
                    ins = mm(ps[2 + k % 2][:, t * P:(t + 1) * P], O1[k % 2][:, t, :],
                             O2[k % 2][:, t, :, :].rearrange("p b j -> p (b j)"), start=True, stop=True)
                ins.then_inc(w_full, 1)

            pe_.wait_ge(h_high_ready, 1)
            pe_.wait_ge(h_low_ready, 1)
            with pe_.Fori(0, 8) as it:
                for k in range(8):
                    down(it, k)
            pe_.wait_ge(sel_ready, 1)
            for k in range(3):
                for t in range(NT):
                    ins = nc.tensor.transpose(ps[4 + k][:, t * P:(t + 1) * P], sel3[:, k, t, :], ident)
            ins.then_inc(selT_full, 1)
            with pe_.Fori(8, 16) as it:
                for k in range(8):
                    down(it, k)
                    weights(it * 8 + (k - 64), k)
            pe_.wait_ge(selT_ready, 3)

            def up(it, k, first=False, last=False):
                outs = [(ps[4 + 2 * t + half][:, :], slice(t * P, (t + 1) * P), slice(half * 512, (half + 1) * 512))
                        for t in range(NT) for half in range(2)]
                g, w = gs[k % 2], wsplit[:, k % SPLIT]
                pe_.wait_ge(gs_high, it * 8 + (k + 1))
                pe_.wait_ge(high_ready, it * 8 + (P + k + 1))
                for o, tok, cols in outs:
                    mm(o, g[0][:, tok], w[:, 0, cols], start=first, stop=False, skip_group_check=True)
                pe_.wait_ge(gs_low, it * 8 + (k + 1))
                for o, tok, cols in outs:
                    mm(o, g[1][:, tok], w[:, 0, cols], start=False, stop=False, skip_group_check=True)
                pe_.wait_ge(low_ready, it * 8 + (P + k + 1))
                for o, tok, cols in outs:
                    ins = mm(o, g[0][:, tok], w[:, 1, cols], start=False, stop=last, skip_group_check=True)
                ins.then_inc(col_done, 1)

            for k in range(8):
                up(0, k, first=(k == 0))
                weights(64 + k, k)
            with pe_.Fori(1, 8) as it:
                for k in range(8):
                    up(it, k)
                    weights(it * 8 + (k + 64), k)
            with pe_.Fori(8, 15) as it:
                for k in range(8):
                    up(it, k)
            for k in range(8):
                up(15, k, last=(k == 7))

        @block.vector
        def _(dve):
            link = chained(dve, dve_chain)
            tt, ts, stt = nc.vector.tensor_tensor, nc.vector.tensor_scalar, nc.vector.scalar_tensor_tensor
            norms = [0]

            def row_sums(xv, scratch):
                for t in range(NT):
                    ins = nc.vector.tensor_tensor_reduce(scratch[:, t, :], xv[:, t, :], xv[:, t, :], 1.0, 0.0, ALU.mult, ALU.add,
                                                         ss[:, t:t + 1])
                link(ins)
                ts(ss, ss, 1.0 / D, EPS, ALU.mult, ALU.add).then_inc(var_ready, 1)
                norms[0] += 1
                dve.wait_ge(rstd_ready, norms[0])

            def normed(b):
                for t in range(NT):
                    ts(xn[b][:, t, :], xv[:, t, :], rstd[:, t:t + 1], None, ALU.mult).then_inc(xn_ready, 1)

            dve.wait_ge(x_in, 16)
            row_sums(xv, xn[0])
            normed(0)
            dve.wait_ge(consts_in, 16 * 8)
            dve.wait_ge(c2_exp, 1)
            link(ts(sc2, sc2, 1.0, None, ALU.add))
            link(nc.vector.reciprocal(sc2, sc2))
            link(tt(sc2, sc2, c2, ALU.mult))

            def rope(s, dst, table_, heads_, half, t, width, lo=0):
                src = bank_read(dve, s)[:, lo:lo + heads_ * width].rearrange("p (h e) -> p h e", h=heads_)
                cos = table_[:, 0, t, :].unsqueeze(1).to_broadcast([P, heads_, half])
                sin = table_[:, 1, t, :].unsqueeze(1).to_broadcast([P, heads_, half])
                rt = ropet[:, 0:heads_ * 2 * half].rearrange("p (b h e) -> p b h e", b=2, h=heads_)
                x1, x2 = src[:, :, 0:half], src[:, :, half:2 * half]
                o1, o2 = dst[:, :, 0:half], dst[:, :, half:2 * half]
                tt(rt[:, 0], x2, sin, ALU.mult)
                tt(o1, x1, cos, ALU.mult)
                tt(rt[:, 1], x1, sin, ALU.mult)
                link(tt(o2, x2, cos, ALU.mult))
                tt(o1, o1, rt[:, 0], ALU.subtract)
                return tt(o2, o2, rt[:, 1], ALU.add)

            def ada(s):
                n = s[1]
                k = ADA.index(n)
                w = wait_panel(dve, n).rearrange("p (c n) -> p c n", c=C)
                cc = c1 if STREAM[n][0] == "ada1" else sc2
                if k >= 2:
                    dve.wait_ge(full[USE[("ada", ADA[k - 2])][0]], USE[("ada", ADA[k - 2])][1])
                a = acc[k % 2]
                link(ts(a, w[:, 0, :], cc[:, 0:1], None, ALU.mult))
                for c in range(1, C):
                    ins = stt(out=a, in0=w[:, c, :], scalar=cc[:, c:c + 1], in1=a, op0=ALU.mult, op1=ALU.add)
                    if c < C - 1:
                        link(ins)
                ins.then_inc(acc_ready, 1)

            def ada_out(s):
                n = s[1]
                name, i = STREAM[n][0], STREAM[n][1]
                src = bank_read(dve, s)
                part, half = divmod(i, 2)
                if name == "ada1":
                    kind, blk_n, bias = ("B", "A", "gate")[part], 0, b1c
                else:
                    kind, blk_n, bias = ("B", "A", "gate")[part % 3], 1 + part // 3, b2c
                if kind == "gate":
                    g = gateB if (name == "ada2" and part == 5) else gateA
                    if name == "ada2" and part == 2 and half == 0:
                        dve.wait_ge(gateA_in, 16)
                    ins = tt(g[:, half * 512:(half + 1) * 512], src[:, :], g[:, half * 512:(half + 1) * 512], ALU.add)
                    bank_free(ins, s)
                    return
                c4 = slice(4 * half, 4 * half + 4)
                bb = bias[:, part * 8 + 4 * half:part * 8 + 4 * half + 4]
                if kind == "B":
                    bank_free(tt(modB[:, blk_n, c4], src[:, 0:4], bb, ALU.add), s)
                    evacuated(dve, s)
                else:
                    ins = tt(modA[:, blk_n, c4], src[:, 0:4], bb, ALU.add)
                    bank_free(ins, s)
                    evacuated(dve, s)
                    link(ts(modA[:, blk_n, c4], modA[:, blk_n, c4], 1.0, None, ALU.add))
                    link(tt(modA[:, blk_n, c4], modA[:, blk_n, c4], gcol[:, blk_n, c4], ALU.mult))

            def head_mask(hh):
                s = ("score", hh)
                src = bank_read(dve, s)
                k = hh % 2
                if hh >= 2:
                    dve.wait_ge(full[USE[("pT", hh - 2)][0]], USE[("pT", hh - 2)][1])
                b = pbuf[k]
                bank_free(tt(b, src[:, 0:384], mask, ALU.add), s)
                evacuated(dve, s)
                nc.vector.tensor_reduce(mx[:, k, 0:1], b[:, 0:P], AX, ALU.max)
                link(nc.vector.tensor_reduce(mx[:, k, 1:2], b[:, P:3 * P], AX, ALU.max))
                ts(nb[:, k, :], mx[:, k, :], -0.125, None, ALU.mult).then_inc(smax, 1)

            def head_norm(hh):
                k = hh % 2
                dve.wait_ge(sexp, hh + 1)
                link(nc.vector.reciprocal(rs[:, k, :], sm[:, k, :]))
                b = pbuf[k]
                h = hh % 8
                gi = None if hh < 8 else 3 * h + (1 if hh < 16 else 2)
                for lo, hi, t in ((0, P, 0), (P, 3 * P, 1)):
                    if gi is None:
                        ins = ts(b[:, lo:hi], b[:, lo:hi], rs[:, k, t:t + 1], None, ALU.mult)
                    else:
                        ins = ts(b[:, lo:hi], b[:, lo:hi], rs[:, k, t:t + 1], egate[:, t, gi:gi + 1], ALU.mult, ALU.mult)
                ins.then_inc(snorm, 1)

            def sigmoid(v):
                link(ts(v, v, 1.0, None, ALU.add))
                link(nc.vector.reciprocal(v, v))

            def merge_sigmoid(i):
                evacuated(dve, ("proj", "in1", i, 1))
                sigmoid(em[:, (i - 6) // 2, :, (i % 2) * 512:(i % 2) * 512 + 512])

            ada_steps = [s for s in STEPS if s[0] == "ada"]
            accs, outs = [0], [0]

            def next_acc(count=1):
                for _ in range(count):
                    if accs[0] < len(ada_steps):
                        ada(ada_steps[accs[0]])
                        accs[0] += 1

            for s in STEPS:
                kind = s[0]
                if s == ("proj", "in1", 2, 0):
                    dve.wait_ge(tables_in, 64)
                if kind == "ada":
                    k = ada_steps.index(s)
                    while accs[0] <= (k + 1 if k < SLOTS - 1 else k):
                        next_acc()
                    ada_out(s)
                    if s == ("ada", AT[("ada1", 1)]):
                        dve.sem_inc(mod_ready, 1)
                elif kind == "xT" and s[2] == 0:
                    b, t, half = s[1:]
                    src = bank_read(dve, s)
                    for c in range(4):
                        cc = 4 * half + c
                        ins = ts(hT[b][:, cc, t * P:(t + 1) * P], src[:, c * P:(c + 1) * P], modA[:, b, cc:cc + 1],
                                 modB[:, b, cc:cc + 1], ALU.mult, ALU.add)
                    bank_free(ins, s)
                elif kind == "proj" and s[1] == "in1" and s[2] in (2, 3):
                    _, _, i, t = s
                    dst = qk_nat[:, i - 2, t, :].rearrange("p (h e) -> p h e", h=H)
                    rope(s, dst, rope1, H, 8, t, 64)
                    src = ps[USE[s][0]][:, :].rearrange("p (h e) -> p h e", h=H)
                    bank_free(nc.vector.tensor_copy(dst[:, :, 16:64], src[:, :, 16:64]), s)
                    evacuated(dve, s)
                elif kind == "proj" and s[1] == "in1" and s[3] == 1 and s[2] in (0, 6):
                    e, z, i = (eza, za, 5) if s[2] == 0 else (ezp, zp, 1)
                    evacuated(dve, ("proj", "in1", i, 1))
                    sigmoid(e)
                    link(tt(z, z, e, ALU.mult))
                elif kind == "proj" and s[1] == "in1" and s[3] == 1 and s[2] > 6:
                    merge_sigmoid(s[2] - 1)
                elif kind == "proj" and s[1] == "in2" and s[2] in (0, 1):
                    _, _, i, t = s
                    ins = rope(s, qk_nat[:, i, t, :].rearrange("p (h e) -> p h e", h=4), ropeR, 4, 64, t, P)
                    bank_free(ins, s)
                    evacuated(dve, s)
                elif kind == "proj" and s[1] == "in2" and s[2] == 4:
                    t = s[3]
                    ins = rope(s, nq_nat[:, t, :].rearrange("p (h e) -> p h e", h=H), ropeN, H, 32, t, 64)
                    bank_free(ins, s)
                    evacuated(dve, s)
                elif kind == "proj" and s[1] == "in2" and s[2] == 5:
                    t = s[3]
                    for w in (0, 2):
                        link(rope(s, kv_nat[:, t, w, :].rearrange("p (h e) -> p h e", h=2), ropeN, 2, 32, t, 64, w * P))
                    src = ps[USE[s][0]]
                    nc.vector.tensor_copy(kv_nat[:, t, 1, :], src[:, P:2 * P])
                    bank_free(nc.vector.tensor_copy(kv_nat[:, t, 3, :], src[:, 3 * P:4 * P]), s)
                elif kind == "proj" and s[1] == "in2b":
                    t = s[3]
                    link(rope(s, kv_nat[:, t, 4, :].rearrange("p (h e) -> p h e", h=2), ropeN, 2, 32, t, 64, 0))
                    src = ps[USE[s][0]]
                    nc.vector.tensor_copy(kv_nat[:, t, 5, :], src[:, P:2 * P])
                    bank_free(nc.vector.tensor_copy(egate[:, t, :], src[:, 2 * P:2 * P + 24]), s)
                elif kind == "hid":
                    kv = s[1]
                    evacuated(dve, ("kvT", kv))
                    for g in range(2):
                        srcg = kvT[:, kv, g, :].rearrange("p (n l) -> p l n", l=2)[:, 0, :]
                        for half in range(2):
                            srcv = srcg[:, 8 * half:8 * half + 8 * NCMP].rearrange("p (n i) -> p i n", i=8)
                            dst = blk[:, kv, 8 * half:8 * half + 8, g * NCMP:(g + 1) * NCMP]
                            pev = pe[:, kv, 8 * half:8 * half + 8].unsqueeze(2).to_broadcast([P, 8, NCMP])
                            ins = tt(dst, srcv, pev, ALU.add)
                    ins.then_inc(blk_ready, 1)
                elif kind == "cmpVrep":
                    src = bank_read(dve, s)[:, 0:P].rearrange("p (g e) -> p g e", g=2)
                    for g in range(2):
                        ins = tt(vbd[:, 4 * g:4 * g + 4, :], src[:, g, :].unsqueeze(1).to_broadcast([P, 4, 64]),
                                 table("bmask")[:, 4 * g:4 * g + 4].unsqueeze(2).to_broadcast([P, 4, 64]), ALU.mult)
                    bank_free(ins, s)
                elif kind == "cmpS":
                    t = s[1]
                    src = bank_read(dve, s)[:, 0:H * NCMP].rearrange("p (h n) -> p h n", h=H)
                    if t == 0:
                        link(nc.vector.memset(pc, 0.0))
                    bank_free(tt(cmps[:, t], src, cmpadd[:, t, :].unsqueeze(1).to_broadcast([P, H, NCMP]), ALU.add), s)
                    evacuated(dve, s)
                    link(nc.vector.tensor_reduce(cm, cmps[:, t], AX, ALU.max))
                    ins = tt(cmps[:, t], cmps[:, t], cm.unsqueeze(2).to_broadcast([P, H, NCMP]), ALU.subtract)
                    if t == 0:
                        link(ins)
                        dve.wait_ge(cmpe, 1)
                        sigmoid(egate)
                    else:
                        ins.then_inc(cmp_ready, 1)
                        dve.wait_ge(cmpe, 2)
                        for tq in range(NT):
                            link(tt(cmps[:, tq], cmps[:, tq], cmpok[:, tq, :].unsqueeze(1).to_broadcast([P, H, NCMP]), ALU.mult))
                            link(nc.vector.tensor_reduce(cs, cmps[:, tq], AX, ALU.add))
                            link(ts(cs, cs, float(np.finfo(np.float32).tiny), None, ALU.max))
                            link(nc.vector.reciprocal(cs, cs))
                            g0 = egate[:, tq, :].rearrange("p (h b) -> p h b", b=3)[:, :, 0]
                            link(tt(cs, cs, g0, ALU.mult))
                            link(tt(pc[:, tq, :, 0:NCMP], cmps[:, tq], cs.unsqueeze(2).to_broadcast([P, H, NCMP]), ALU.mult))
                        dve.sem_inc(cmpp, 1)
                elif kind == "score":
                    head_mask(s[1])
                    if s[1] % 8:
                        head_norm(s[1] - 1)
                    if s[1] % 8 == 7:
                        head_norm(s[1])
                elif kind == "ret":
                    h = s[1]
                    src = bank_read(dve, s)
                    if h >= 2:
                        dve.wait_ge(ret_done, h - 1)
                    bank_free(tt(rpt[h % 2], src[:, 0:384], decay[:, h, :], ALU.mult), s)
                    evacuated(dve, s)
                    dve.sem_inc(ret_p, 1)
                elif kind == "poolT" and s[1] == 0:
                    merge_sigmoid(9)
                    dve.wait_ge(pv_done, 8)
                    for t in range(NT):
                        tt(za[:, t, :], ps[6 + t][:, :], za[:, t, :], ALU.mult).then_inc(y_ready, 1)
                    dve.wait_ge(y_ready, NT)
                    dve.sem_inc(o_freed, 2)
                elif kind == "pool":
                    t = s[1]
                    src = bank_read(dve, s)
                    if t == 0:
                        dve.wait_ge(band_in, 48)
                    bank_free(tt(ezp[:, t, :], src[:, :], pscale, ALU.mult), s)
                    evacuated(dve, s)
                    tt(zp[:, t, :], ezp[:, t, :], zp[:, t, :], ALU.mult).then_inc(y_ready, 1)
                elif kind == "up":
                    _, name, t, half = s
                    src = bank_read(dve, s)
                    c = slice(half * 512, (half + 1) * 512)
                    if name == "poolup":
                        bank_free(tt(merged[0][:, t, c], src[:, :], em[:, 0, t, c], ALU.mult), s)
                    else:
                        bank_free(tt(em[:, 1, t, c], src[:, :], em[:, 1, t, c], ALU.mult), s)
                        evacuated(dve, s)
                        link(tt(merged[0][:, t, c], merged[0][:, t, c], em[:, 1, t, c], ALU.add))
                        if half == 1:
                            dve.sem_inc(merged_ready, 1)
                elif kind == "wout":
                    _, b, half, t = s
                    src = bank_read(dve, s)
                    c = slice(half * 512, (half + 1) * 512)
                    sc = tmp(9216, 512)
                    bank_free(tt(sc, src[:, :], gateA[:, c], ALU.mult), s)
                    evacuated(dve, s)
                    link(tt(xv[:, t, c], xv[:, t, c], sc, ALU.add))
                    if half == 1 and t == 1:
                        if b == 0:
                            row_sums(xv, xn[1])
                            for q in range(NT):
                                link(stt(out=xv[:, q, :], in0=xv[:, q, :], scalar=rstd[:, q:q + 1], in1=gfin,
                                         op0=ALU.mult, op1=ALU.mult))
                            dve.sem_inc(x_ready, 1)
                        row_sums(xv, xn[1])
                        normed(1 + b)
                        dve.sem_inc(mod_ready, 1)
                        if b == 1:
                            dve.sem_inc(ring_free, 1)
                elif kind == "cmpO" and s[1] == 1:
                    for t in range(NT):
                        dve.wait_ge(o_full, t + 1)
                        tc = nc.vector.tensor_copy(merged[1][:, t, 512:D], ps[6 + t][:, :])
                        tc.then_inc(merged_ready, 1)
                    dve.sem_inc(o_freed, 2)
                elif s in (("retO", 1), ("retO", 3)):
                    t = s[1] // 2
                    evacuated(dve, ("proj", "in2", 3, t))
                    sigmoid(eza[:, t, :])
                    link(tt(za[:, t, :], za[:, t, :], eza[:, t, :], ALU.mult))
                elif s == ("pT", 21):
                    dve.wait_ge(ret_done, 4)
                    for t in range(NT):
                        for h in range(4):
                            link(nc.vector.bn_stats(bst, ps[4 + t][:, h * P:(h + 1) * P]))
                            link(nc.vector.bn_aggr(bnv[:, t, h, :], bst))
                    ts(cs.rearrange("p (t h) -> p t h", t=NT), bnv[:, :, :, 1], EPS, None, ALU.add).then_inc(gn_var, 1)
                elif s == ("pT", 22):
                    dve.wait_ge(gn_rstd, 1)
                    for t in range(NT):
                        for h in range(4):
                            ins = ts(merged[1][:, t, h * P:(h + 1) * P], ps[4 + t][:, h * P:(h + 1) * P], bnv[:, t, h, 0:1],
                                     rr[:, 4 * t + h:4 * t + h + 1], ALU.subtract, ALU.mult)
                        link(ins)
                        link(tt(merged[1][:, t, 0:512], merged[1][:, t, 0:512], za[:, t, :], ALU.mult))
                if kind == "proj":
                    ahead = [a for a in ada_steps if a[1] < AT[(s[1], s[2])] + 3]
                    due = max(len(ahead) - accs[0], 0)
                    next_acc(min(due, 1) if s[3] == 0 else due)

            dve.wait_ge(h_high_ready, 1)
            for k in range(8):
                evacuated(dve, ("peerq", k))
            tt(h_low, hT[2], h_high.bitcast(F32), ALU.subtract).then_inc(h_low_ready, 1)

            for k in range(8):
                evacuated(dve, ("peers", k))

            def top16(values, best, where):
                link(nc.vector.max(best[:, 0:8], values))
                link(nc.vector.max_index(where[:, 0:8], best[:, 0:8], values))
                link(nc.vector.match_replace(values, best[:, 0:8], values, LOWEST))
                link(nc.vector.max(best[:, 8:16], values))
                link(nc.vector.max_index(where[:, 8:16], best[:, 8:16], values))

            iu, ju, ju2 = i16u.bitcast(U32), tju.bitcast(U32), tju2.bitcast(U32)
            for t in range(NT):
                for g in range(16):
                    top16(s_all[:, t, g, :], v16[:, t, g, :], iu[:, t, g, :])
                link(nc.vector.tensor_copy(i16f[:, t], iu[:, t]))
                vv = v16[:, t].rearrange("p (h b) k -> p h b k", b=2)
                ff = i16f[:, t].rearrange("p (h b) k -> p h b k", b=2)
                first = vv[:, :, 0, :].unsqueeze(3).to_broadcast([P, H, K16, K16])
                second = vv[:, :, 1, :].unsqueeze(2).to_broadcast([P, H, K16, K16])
                link(tt(cand, first, second, ALU.add))
                for h in range(H):
                    top16(cand[:, h].rearrange("p a b -> p (a b)"), tv[:, h, :], ju[:, h, :])
                link(ts(ju2, ju, 15, None, ALU.bitwise_and))
                link(nc.vector.tensor_copy(taf[:, 1], ju2))
                link(ts(ju2, ju, 4, None, ALU.logical_shift_right))
                link(nc.vector.tensor_copy(taf[:, 0], ju2))
                for b in range(2):
                    rank = taf[:, b].unsqueeze(3).to_broadcast([P, H, K16, K16])
                    ranks = iota[:, 0:16].unsqueeze(1).unsqueeze(1).to_broadcast([P, H, K16, K16])
                    link(tt(eq, rank, ranks, ALU.is_equal))
                    link(tt(eq, eq, ff[:, :, b, :].unsqueeze(2).to_broadcast([P, H, K16, K16]), ALU.mult))
                    link(nc.vector.tensor_reduce(sel3[:, b, t, :].rearrange("p (h k) -> p h k", h=H), eq, AX, ALU.add))
                w = sel3[:, 2, t, :].rearrange("p (h k) -> p h k", h=H)
                link(tt(w, tv, tv[:, :, 0:1].to_broadcast([P, H, K16]), ALU.subtract))
            dve.sem_inc(wexp_in, 1)
            dve.wait_ge(wexp, 1)
            for t in range(NT):
                w = sel3[:, 2, t, :].rearrange("p (h k) -> p h k", h=H)
                link(nc.vector.tensor_reduce(sm8, w, AX, ALU.add))
                link(nc.vector.reciprocal(sm8, sm8))
                link(tt(w, w, sm8.unsqueeze(2).to_broadcast([P, H, K16]), ALU.mult))
            dve.sem_inc(sel_ready, 1)
            dve.wait_ge(selT_full, 1)
            for k in range(2):
                nc.vector.tensor_copy(selT[:, k, :], ps[4 + k][:, 0:T])
            nc.vector.tensor_copy(selT[:, 2, :].bitcast(F32R), ps[6][:, 0:T]).then_inc(selT_ready, 1)
            dve.wait_ge(selT_ready, 1)
            tt(selT[:, 3, :], ps[6][:, 0:T], selT[:, 2, :], ALU.subtract).then_inc(selT_ready, 2)
            dve.wait_ge(selT_ready, 3)
            for k in range(2):
                nc.vector.memset(dummy[:, 4 + k:5 + k], 0.0).then_inc(w_credit, 1)

            def build(b, m, k, chunk):
                at = bass.ds(b * 4, 4)
                wide = lambda row, n: selT[:, row, at].unsqueeze(2).to_broadcast([P, 4, n])
                keys = iota[:, 64 * chunk:64 * chunk + 64].unsqueeze(1).to_broadcast([P, 4, 64])
                if not (isinstance(m, int) and m == 0):
                    dve.wait_ge(hot_ready, m)
                tt(hot2, keys, wide(1, 64), ALU.is_equal).then_inc(hot2_ready, 1)
                tt(O1[k], iota.unsqueeze(1).to_broadcast([P, 4, P]), wide(0, P), ALU.is_equal)
                dve.wait_ge(hot2_ready, m + 1)
                tt(O2[k][:, :, 0, :], hot2, wide(2, 64), ALU.mult)
                tt(O2[k][:, :, 1, :], hot2, wide(3, 64), ALU.mult).then_inc(hot_ready, 1)

            def weigh(b, m, k, chunk):
                dve.wait_ge(w_copied, m + 1)
                low = ps[2 + k][:, :].rearrange("p (t b j) -> p t b j", t=4, b=2)[:, :, 1, :]
                tt(wsum[k], low, wsum[k], ALU.add).then_inc(w_credit, 1)
                g = Gv[:, 64 * chunk:64 * chunk + 64, bass.ds(b * 4, 4)]
                dve.wait_ge(w_credit, m + 3)
                tt(g, wsum[k].rearrange("p t j -> p j t"), g, ALU.mult).then_inc(w_done, 1)

            def gs_lower(j, k):
                dve.wait_ge(gs_high, j + 1)
                tt(gs[k][1].unsqueeze(1), Gv[:, bass.ds(j, 1), :], gs[k][0].bitcast(F32).unsqueeze(1), ALU.subtract)\
                    .then_inc(gs_low, 1)

            dve.sem_inc(w_done, 2)
            for k in range(2):
                build(k, k, k, 0)
            dve.wait_ge(act_credit, 2 + 64)
            with dve.Fori(0, 31) as it:
                for k in range(2):
                    weigh(it * 2 + k, it * 2 + k, k, 0)
                    build(it * 2 + (k + 2), it * 2 + (k + 2), k, 0)
            for k in range(2):
                weigh(62 + k, 62 + k, k, 0)
                build(k, 64 + k, k, 1)
            for k in range(2):
                gs_lower(k, k)
            dve.wait_ge(act_credit, 2 + 128)
            with dve.Fori(0, 31) as it:
                for k in range(2):
                    gs_lower(it * 2 + (k + 2), k)
                    weigh(it * 2 + k, it * 2 + (64 + k), k, 1)
                    build(it * 2 + (k + 2), it * 2 + (66 + k), k, 1)
            for k in range(2):
                weigh(62 + k, 126 + k, k, 1)
            with dve.Fori(8, 16) as it:
                for k in range(8):
                    dve.wait_ge(high_ready, it * 8 + (P + k + 1))
                    tt(wsplit[:, k % SPLIT, 1, :], raw[:, k % RAW, :], wsplit[:, k % SPLIT, 0, :].bitcast(F32), ALU.subtract)\
                        .then_inc(low_ready, 1)
                    gs_lower(it * 8 + k, k % 2)

            dve.wait_ge(col_done, 2 * P)
            dve.wait_ge(x_reloaded, 32)
            for t in range(NT):
                for half in range(2):
                    c = slice(half * 512, (half + 1) * 512)
                    ins = tt(fin[:, t, c], ps[4 + 2 * t + half][:, :], gateB[:, c], ALU.mult)
            link(ins)
            for t in range(NT):
                ins = tt(x_back[:, t, :], x_back[:, t, :], fin[:, t, :], ALU.add)
            link(ins)
            row_sums(x_back, fin)
            for t in range(NT):
                stt(out=fin[:, t, :], in0=x_back[:, t, :], scalar=rstd[:, t:t + 1], in1=gfin2, op0=ALU.mult, op1=ALU.mult)\
                    .then_inc(out_ready, 1)


def kernel(**inputs):
    import concourse.bacc as bacc
    from concourse.bass_utils import run_bass_kernel_spmd

    a = {k: np.asarray(v) for k, v in inputs.items()}
    tab, keep, band, offsets = tables()

    def panels(w, width=512):
        k, n = w.shape
        return w.reshape(k // P, P, n // width, width).transpose(2, 1, 0, 3).reshape(n // width, P, -1)

    def columns(v):
        return v.reshape(-1, P).T

    in2, b1, b2 = a["w_in_2"][0], a["b_ada"][0], a["b_ada_2"][0]
    arrays = {
        "x": a["x"][0].reshape(NT, P, D).transpose(1, 0, 2),
        "tab": tab, "keep": keep, "band": band,
        "c1": columns(a["c"][0]), "c2": columns(a["c_2"][0]),
        "b1": columns(b1), "b2": columns(b2),
        "gate1": b1[2 * D:], "gate2": b2[2 * D:3 * D], "gate3": b2[5 * D:],
        "gfin1": a["g_final"], "gfin2": a["g_norm_final_2"],
        "g": np.concatenate([columns(a[k][0]) for k in ("g_norm", "g_norm_mix_2", "g_norm_ffn_2")], 1),
        "pe": np.concatenate([columns(a[k][0].reshape(-1)) for k in ("pe_cmp_k_2", "pe_cmp_v_2")], 1),
        "cb1": np.concatenate([columns(a[k][0]) for k in ("b_cmp_k1_2", "b_cmp_v1_2")], 1),
        "w2k": np.concatenate([a["w_cmp_k2_2"][0].reshape(2, P, 64).transpose(1, 0, 2)] * 2, 2),
        "w2v": a["w_cmp_v2_2"][0].reshape(2, P, 64).transpose(1, 0, 2),
        "wgrp": a["w_pool_grp"][0].transpose(1, 0, 2).reshape(P, -1),
        "pscale": a["pool_scale"][0],
        "ada1": panels(a["w_ada"][0]), "in1": panels(a["w_in"][0]),
        "poolup": a["w_pool_up"][0].reshape(4, P, D).transpose(1, 0, 2).reshape(P, -1),
        "attnup": a["w_attn_up"][0].reshape(4, P, D).transpose(1, 0, 2).reshape(P, -1),
        "out1": panels(a["w_out"][0]), "ada2": panels(a["w_ada_2"][0]),
        "in2": panels(in2[:, :3072]), "in2b": panels(in2[:, 3072:], 280)[0],
        "cmpk": a["w_cmp_k1_2"][0].reshape(16, P, 256).transpose(1, 0, 2).reshape(P, -1),
        "cmpv": a["w_cmp_v1_2"][0].reshape(16, P, 256).transpose(1, 0, 2).reshape(P, -1),
        "out2": panels(a["w_out_2"][0]), "wq": panels(a["w_peer_q_2"][0]),
        "subkeys": a["peer_subkeys_2"][0].transpose(3, 0, 1, 2).reshape(P, -1),
        "down": a["peer_down_2"][0].reshape(P, P, C, P).transpose(1, 3, 2, 0).reshape(P, P, -1),
        "up": a["peer_up_2"][0].reshape(P, P, D).transpose(1, 0, 2),
    }
    nc = bacc.Bacc("TRN2", target_bir_lowering=False, num_devices=1)
    sent, d = {}, {"offsets": offsets}
    for name, v in arrays.items():
        v = np.ascontiguousarray(v)
        sent[f"in_{name}"] = v
        d[name] = nc.dram_tensor(f"in_{name}", v.shape, mybir.dt.from_np(v.dtype), kind="ExternalInput").ap()
    out = nc.dram_tensor("out_0", (P, NT, D), F32, kind="ExternalOutput").ap()
    program(nc, d, out)
    r = run_bass_kernel_spmd(nc, [sent], core_ids=[0])
    return r.results[0]["out_0"].transpose(1, 0, 2).reshape(1, T, D)
```
